# Optimizing a Trainium2 kernel written in Bass

```python
import math
import jax, jax.numpy as jnp
from jax import lax
import numpy as np

D_MODEL = 1024
BATCH = 1
SEQ = 256
DEPTH = 2

N_MIXERS = 2
GRID_W = 64
Q_BLOCK = 128
EPS = 1e-6

A_HEAD_DIM = 64
A_N_HEADS = D_MODEL // (2 * A_HEAD_DIM)
A_ROT = A_HEAD_DIM // 4
ROPE_THETA_1D = 500000.0

B_HEAD_DIM = 128
B_N_HEADS = D_MODEL // B_HEAD_DIM
B_N_KV = max(1, B_N_HEADS // 4)
B_GROUP = B_N_HEADS // B_N_KV
ROPE_THETA_AXIAL = 10000.0

D_FF = -(-8 * D_MODEL // (3 * 256)) * 256

N_A_LAYERS = (DEPTH + 1) // 2
N_B_LAYERS = DEPTH // 2


def rmsnorm(x, g):
    xf = x.astype(jnp.float32)
    y = xf * lax.rsqrt(jnp.mean(xf * xf, axis=-1, keepdims=True) + EPS)
    return (y * g.astype(jnp.float32)).astype(x.dtype)

def rope_angles(pos, dim, theta):
    half = dim // 2
    freqs = theta ** (-jnp.arange(half, dtype=jnp.float32) / half)
    ang = pos.astype(jnp.float32)[:, None] * freqs[None, :]
    return jnp.cos(ang), jnp.sin(ang)

def apply_rope(x, cos, sin):
    shape = (1, x.shape[1]) + (1,) * (x.ndim - 3) + (cos.shape[-1],)
    c = cos.reshape(shape).astype(x.dtype)
    s = sin.reshape(shape).astype(x.dtype)
    x1, x2 = jnp.split(x, 2, axis=-1)
    return jnp.concatenate([x1 * c - x2 * s, x2 * c + x1 * s], axis=-1)

def lambda_init_fn(layer_idx):
    return 0.8 - 0.6 * math.exp(-0.3 * layer_idx)

def diff_attention(h, w_qkv, w_o, lq1, lk1, lq2, lk2, subln_g, lam_init, cos, sin):
    B_, S, _ = h.shape
    qkv = h @ w_qkv
    q, k, v = jnp.split(qkv, 3, axis=-1)
    q = q.reshape(B_, S, A_N_HEADS, 2, A_HEAD_DIM)
    k = k.reshape(B_, S, A_N_HEADS, 2, A_HEAD_DIM)
    v = v.reshape(B_, S, A_N_HEADS, 2 * A_HEAD_DIM)
    q = jnp.concatenate([apply_rope(q[..., :A_ROT], cos, sin), q[..., A_ROT:]], axis=-1)
    k = jnp.concatenate([apply_rope(k[..., :A_ROT], cos, sin), k[..., A_ROT:]], axis=-1)
    q = q * (A_HEAD_DIM ** -0.5)
    lam = (jnp.exp(jnp.sum(lq1.astype(jnp.float32) * lk1.astype(jnp.float32)))
           - jnp.exp(jnp.sum(lq2.astype(jnp.float32) * lk2.astype(jnp.float32)))
           + lam_init)
    nb = S // Q_BLOCK
    qb = q.reshape(B_, nb, Q_BLOCK, A_N_HEADS, 2, A_HEAD_DIM).transpose(1, 0, 2, 3, 4, 5)

    def block(qi):
        s = jnp.einsum('bqhcd,bkhcd->bhcqk', qi, k).astype(jnp.float32)
        p = jax.nn.softmax(s, axis=-1)
        w = (p[:, :, 0] - lam * p[:, :, 1]).astype(v.dtype)
        return jnp.einsum('bhqk,bkhe->bqhe', w, v)

    o = lax.map(block, qb)
    o = o.transpose(1, 0, 2, 3, 4).reshape(B_, S, A_N_HEADS, 2 * A_HEAD_DIM)
    o = rmsnorm(o, subln_g) * (1.0 - lam_init)
    return o.reshape(B_, S, A_N_HEADS * 2 * A_HEAD_DIM) @ w_o

def axial_gqa(h, w_qkv, w_o, qnorm_g, knorm_g, cos_r, sin_r, cos_c, sin_c):
    B_, S, _ = h.shape
    qkv = h @ w_qkv
    nq = B_N_HEADS * B_HEAD_DIM
    nkv = B_N_KV * B_HEAD_DIM
    q = qkv[..., :nq].reshape(B_, S, B_N_HEADS, B_HEAD_DIM)
    k = qkv[..., nq:nq + nkv].reshape(B_, S, B_N_KV, B_HEAD_DIM)
    v = qkv[..., nq + nkv:].reshape(B_, S, B_N_KV, B_HEAD_DIM)
    q = rmsnorm(q, qnorm_g)
    k = rmsnorm(k, knorm_g)
    half = B_HEAD_DIM // 2
    q = jnp.concatenate([apply_rope(q[..., :half], cos_r, sin_r), apply_rope(q[..., half:], cos_c, sin_c)], axis=-1)
    k = jnp.concatenate([apply_rope(k[..., :half], cos_r, sin_r), apply_rope(k[..., half:], cos_c, sin_c)], axis=-1)
    q = (q * (B_HEAD_DIM ** -0.5)).reshape(B_, S, B_N_KV, B_GROUP, B_HEAD_DIM)
    nb = S // Q_BLOCK
    qb = q.reshape(B_, nb, Q_BLOCK, B_N_KV, B_GROUP, B_HEAD_DIM).transpose(1, 0, 2, 3, 4, 5)

    def block(qi):
        s = jnp.einsum('bqhgd,bkhd->bhgqk', qi, k).astype(jnp.float32)
        p = jax.nn.softmax(s, axis=-1).astype(v.dtype)
        return jnp.einsum('bhgqk,bkhd->bqhgd', p, v)

    o = lax.map(block, qb)
    o = o.transpose(1, 0, 2, 3, 4, 5).reshape(B_, S, nq)
    return o @ w_o

def swiglu(h, w_in, w_out):
    gate, up = jnp.split(h @ w_in, 2, axis=-1)
    return (jax.nn.silu(gate) * up) @ w_out

def first_inputs(seed: int = 0) -> dict:
    key = jax.random.key(seed)
    ks = jax.random.split(key, 24)
    f32 = jnp.float32
    D = D_MODEL
    nrm = lambda k, shape, s: jax.random.normal(k, shape, f32) * s
    b_qkv_out = B_N_HEADS * B_HEAD_DIM + 2 * B_N_KV * B_HEAD_DIM
    return {
        "x": nrm(ks[0], (BATCH, SEQ, D), 1.0),
        "c": nrm(ks[1], (BATCH, D), 1.0),
        "ada_w": nrm(ks[2], (DEPTH, D, 6 * D), 0.5 * D ** -0.5),
        "ada_b": nrm(ks[3], (DEPTH, 6 * D), 0.01),
        "norm1_g": 1.0 + nrm(ks[4], (DEPTH, D), 0.02),
        "norm2_g": 1.0 + nrm(ks[5], (DEPTH, D), 0.02),
        "a_w_qkv": nrm(ks[6], (N_A_LAYERS, D, 3 * D), D ** -0.5),
        "a_w_o": nrm(ks[7], (N_A_LAYERS, D, D), D ** -0.5),
        "a_lam_q1": nrm(ks[8], (N_A_LAYERS, A_HEAD_DIM), 0.1),
        "a_lam_k1": nrm(ks[9], (N_A_LAYERS, A_HEAD_DIM), 0.1),
        "a_lam_q2": nrm(ks[10], (N_A_LAYERS, A_HEAD_DIM), 0.1),
        "a_lam_k2": nrm(ks[11], (N_A_LAYERS, A_HEAD_DIM), 0.1),
        "a_subln_g": 1.0 + nrm(ks[12], (N_A_LAYERS, 2 * A_HEAD_DIM), 0.02),
        "b_w_qkv": nrm(ks[13], (N_B_LAYERS, D, b_qkv_out), D ** -0.5),
        "b_w_o": nrm(ks[14], (N_B_LAYERS, B_N_HEADS * B_HEAD_DIM, D), (B_N_HEADS * B_HEAD_DIM) ** -0.5),
        "b_qnorm_g": 1.0 + nrm(ks[15], (N_B_LAYERS, B_HEAD_DIM), 0.02),
        "b_knorm_g": 1.0 + nrm(ks[16], (N_B_LAYERS, B_HEAD_DIM), 0.02),
        "f_w_in": nrm(ks[17], (DEPTH, D, 2 * D_FF), D ** -0.5),
        "f_w_out": nrm(ks[18], (DEPTH, D_FF, D), D_FF ** -0.5),
        "final_g": 1.0 + nrm(ks[19], (D,), 0.02),
    }

def first_block(x, c, ada_w, ada_b, norm1_g, norm2_g, a_w_qkv, a_w_o, a_lam_q1, a_lam_k1,
              a_lam_q2, a_lam_k2, a_subln_g, b_w_qkv, b_w_o, b_qnorm_g, b_knorm_g,
              f_w_in, f_w_out, final_g):
    S = x.shape[1]
    rows = S // GRID_W
    t = jnp.arange(S, dtype=jnp.int32)
    row_pos = jnp.broadcast_to(jnp.arange(rows, dtype=jnp.int32)[:, None], (rows, GRID_W)).reshape(S)
    col_pos = jnp.broadcast_to(jnp.arange(GRID_W, dtype=jnp.int32)[None, :], (rows, GRID_W)).reshape(S)
    cos_a, sin_a = rope_angles(t, A_ROT, ROPE_THETA_1D)
    cos_r, sin_r = rope_angles(row_pos, B_HEAD_DIM // 2, ROPE_THETA_AXIAL)
    cos_c, sin_c = rope_angles(col_pos, B_HEAD_DIM // 2, ROPE_THETA_AXIAL)
    cond = jax.nn.silu(c)

    for i in range(DEPTH):
        mod = (cond @ ada_w[i] + ada_b[i])[:, None, :]
        shift1, scale1, gate1, shift2, scale2, gate2 = jnp.split(mod, 6, axis=-1)
        h = rmsnorm(x, norm1_g[i]) * (1.0 + scale1) + shift1
        j = i // N_MIXERS
        if i % N_MIXERS == 0:
            y = diff_attention(h, a_w_qkv[j], a_w_o[j], a_lam_q1[j], a_lam_k1[j],
                               a_lam_q2[j], a_lam_k2[j], a_subln_g[j],
                               lambda_init_fn(i), cos_a, sin_a)
        else:
            y = axial_gqa(h, b_w_qkv[j], b_w_o[j], b_qnorm_g[j], b_knorm_g[j],
                          cos_r, sin_r, cos_c, sin_c)
        x = x + gate1 * y
        h = rmsnorm(x, norm2_g[i]) * (1.0 + scale2) + shift2
        x = x + gate2 * swiglu(h, f_w_in[i], f_w_out[i])

    return rmsnorm(x, final_g)


DEPTH_2 = 1

GMLP_WIDTH = 768
GMLP_GROUPS = 4
GMLP_GROUP_DIM = GMLP_WIDTH // GMLP_GROUPS
GMLP_CHUNK = 128
HEAD_DIM = 64
HEADS_PER_GROUP = 4
DILATED_GROUPS = ((128, 1), (512, 4), (2048, 16))
N_ATTN_GROUPS = 3
N_ATTN_HEADS = N_ATTN_GROUPS * HEADS_PER_GROUP
ATTN_WIDTH = N_ATTN_HEADS * HEAD_DIM
ATTN_OUT_WIDTH = HEADS_PER_GROUP * HEAD_DIM
ATTN_BLOCK = 128
ROPE_THETA = 500000.0
ROT_DIM = HEAD_DIM // 4
N_BRANCHES = 2
IN_WIDTH = 2 * GMLP_WIDTH + 3 * ATTN_WIDTH + N_BRANCHES * D_MODEL
D_FF_2 = 2816
CONV_WIDTH = 3


def rms_norm(x, g):
    xf = x.astype(jnp.float32)
    y = xf * lax.rsqrt(jnp.mean(xf * xf, axis=-1, keepdims=True) + EPS)
    return (y * g.astype(jnp.float32)).astype(x.dtype)

def apply_partial_rope(t, cos, sin):
    half = ROT_DIM // 2
    rot = t[..., :ROT_DIM].astype(jnp.float32)
    t1, t2 = rot[..., :half], rot[..., half:]
    rotated = jnp.concatenate([t1 * cos - t2 * sin, t1 * sin + t2 * cos], axis=-1)
    return jnp.concatenate([rotated.astype(t.dtype), t[..., ROT_DIM:]], axis=-1)

def chunked_spatial_gating(z, norm_g, w_s, b_s):
    b, s, _ = z.shape
    u, v = z[..., :GMLP_WIDTH], z[..., GMLP_WIDTH:]
    v = rms_norm(v, norm_g)
    n_chunks = s // GMLP_CHUNK
    vg = v.reshape(b, n_chunks, GMLP_CHUNK, GMLP_GROUPS, GMLP_GROUP_DIM)
    causal = jnp.tril(jnp.ones((GMLP_CHUNK, GMLP_CHUNK), dtype=bool))
    w = jnp.where(causal[None], w_s, jnp.zeros_like(w_s))
    mixed = jnp.einsum('gts,bcsgd->bctgd', w, vg) + b_s.T[None, None, :, :, None]
    return u * mixed.reshape(b, s, GMLP_WIDTH)

def banded_window_attention(q, k, v, steps):
    n, l, h, dh = q.shape
    nb = -(-l // ATTN_BLOCK)
    pad = nb * ATTN_BLOCK - l

    def blocks(t):
        t = jnp.pad(t, ((0, 0), (0, pad), (0, 0), (0, 0)))
        return t.reshape(n, nb, ATTN_BLOCK, h, dh)

    def with_prev(t):
        prev = jnp.pad(t, ((0, 0), (1, 0), (0, 0), (0, 0), (0, 0)))[:, :-1]
        return jnp.concatenate([prev, t], axis=2)

    qb = blocks(q)
    kc = with_prev(blocks(k))
    vc = with_prev(blocks(v))
    scores = jnp.einsum('nbqhd,nbkhd->nbhqk', qb, kc,
                        preferred_element_type=jnp.float32) * (HEAD_DIM ** -0.5)
    qi = jnp.arange(ATTN_BLOCK)[:, None]
    ki = jnp.arange(2 * ATTN_BLOCK)[None, :]
    dist = ATTN_BLOCK + qi - ki
    band = (dist >= 0) & (dist <= steps)
    first_ok = (jnp.arange(nb)[:, None, None] > 0) | (ki[None] >= ATTN_BLOCK)
    valid = band[None] & first_ok
    scores = jnp.where(valid[None, :, None], scores, -jnp.inf)
    m = jnp.max(scores, axis=-1, keepdims=True)
    p = jnp.exp(scores - m)
    den = jnp.sum(p, axis=-1, keepdims=True)
    out = jnp.einsum('nbhqk,nbkhd->nbqhd', (p / den).astype(v.dtype), vc)
    lse = (m + jnp.log(den))[..., 0]
    lse = lse.transpose(0, 1, 3, 2).reshape(n, nb * ATTN_BLOCK, h)[:, :l]
    out = out.reshape(n, nb * ATTN_BLOCK, h, dh)[:, :l]
    return out, lse

def dilated_mixture_attention(q, k, v):
    b, s = q.shape[:2]
    outs, lses = [], []
    for g, (window, dil) in enumerate(DILATED_GROUPS):
        lo, hi = g * HEADS_PER_GROUP, (g + 1) * HEADS_PER_GROUP
        sub = s // dil

        def to_residue(t):
            t = t[:, :, lo:hi].reshape(b, sub, dil, HEADS_PER_GROUP, HEAD_DIM)
            return t.transpose(0, 2, 1, 3, 4).reshape(b * dil, sub, HEADS_PER_GROUP, HEAD_DIM)

        o, lse = banded_window_attention(to_residue(q), to_residue(k), to_residue(v), window // dil)
        o = o.reshape(b, dil, sub, HEADS_PER_GROUP, HEAD_DIM).transpose(0, 2, 1, 3, 4)
        lse = lse.reshape(b, dil, sub, HEADS_PER_GROUP).transpose(0, 2, 1, 3)
        outs.append(o.reshape(b, s, HEADS_PER_GROUP, HEAD_DIM))
        lses.append(lse.reshape(b, s, HEADS_PER_GROUP))
    o_all = jnp.stack(outs, axis=3)
    alpha = jax.nn.softmax(jnp.stack(lses, axis=-1), axis=-1)
    mixed = jnp.einsum('bshg,bshgd->bshd', alpha.astype(o_all.dtype), o_all)
    return mixed.reshape(b, s, ATTN_OUT_WIDTH)

def causal_depthwise_conv(a, w, bias):
    s = a.shape[1]
    a_pad = jnp.pad(a, ((0, 0), (CONV_WIDTH - 1, 0), (0, 0)))
    y = a_pad[:, 0:s] * w[0]
    for j in range(1, CONV_WIDTH):
        y = y + a_pad[:, j:j + s] * w[j]
    return y + bias

def second_inputs(seed: int = 0) -> dict:
    key = jax.random.key(seed)
    ks = jax.random.split(key, 16)
    f32 = jnp.float32
    nrm = lambda k, shape, scale: jax.random.normal(k, shape, f32) * scale
    return {
        "x": nrm(ks[0], (BATCH, SEQ, D_MODEL), 1.0),
        "positions": jnp.broadcast_to(jnp.arange(SEQ, dtype=jnp.int32), (BATCH, SEQ)),
        "mix_norm_g": 1.0 + nrm(ks[1], (DEPTH_2, D_MODEL), 0.02),
        "w_in": nrm(ks[2], (DEPTH_2, D_MODEL, IN_WIDTH), D_MODEL ** -0.5),
        "gmlp_norm_g": 1.0 + nrm(ks[3], (DEPTH_2, GMLP_WIDTH), 0.02),
        "w_spatial": nrm(ks[4], (DEPTH_2, GMLP_GROUPS, GMLP_CHUNK, GMLP_CHUNK), GMLP_CHUNK ** -0.5),
        "b_spatial": 1.0 + nrm(ks[5], (DEPTH_2, GMLP_GROUPS, GMLP_CHUNK), 0.1),
        "w_branch_a": nrm(ks[6], (DEPTH_2, GMLP_WIDTH, D_MODEL), GMLP_WIDTH ** -0.5),
        "w_branch_b": nrm(ks[7], (DEPTH_2, ATTN_OUT_WIDTH, D_MODEL), ATTN_OUT_WIDTH ** -0.5),
        "w_out": nrm(ks[8], (DEPTH_2, D_MODEL, D_MODEL), D_MODEL ** -0.5),
        "ffn_norm_g": 1.0 + nrm(ks[9], (DEPTH_2, D_MODEL), 0.02),
        "w_up": nrm(ks[10], (DEPTH_2, D_MODEL, 2 * D_FF_2), D_MODEL ** -0.5),
        "conv_w": nrm(ks[11], (DEPTH_2, CONV_WIDTH, D_FF_2), CONV_WIDTH ** -0.5),
        "conv_b": nrm(ks[12], (DEPTH_2, D_FF_2), 0.01),
        "w_down": nrm(ks[13], (DEPTH_2, D_FF_2, D_MODEL), D_FF_2 ** -0.5),
        "final_norm_g": 1.0 + nrm(ks[14], (D_MODEL,), 0.02),
    }

def second_block(x, positions, mix_norm_g, w_in, gmlp_norm_g, w_spatial, b_spatial,
              w_branch_a, w_branch_b, w_out, ffn_norm_g, w_up, conv_w, conv_b,
              w_down, final_norm_g):
    b, s, _ = x.shape
    inv_freq = ROPE_THETA ** (-jnp.arange(0, ROT_DIM, 2, dtype=jnp.float32) / ROT_DIM)
    ang = positions.astype(jnp.float32)[..., None] * inv_freq
    cos = jnp.cos(ang)[:, :, None, :]
    sin = jnp.sin(ang)[:, :, None, :]
    splits = [2 * GMLP_WIDTH, 2 * GMLP_WIDTH + ATTN_WIDTH,
              2 * GMLP_WIDTH + 2 * ATTN_WIDTH, 2 * GMLP_WIDTH + 3 * ATTN_WIDTH]
    for layer in range(DEPTH_2):
        h = rms_norm(x, mix_norm_g[layer])
        proj = h @ w_in[layer]
        z_a, q, k, v, gate_logits = jnp.split(proj, splits, axis=-1)
        y_a = chunked_spatial_gating(jax.nn.gelu(z_a, approximate=False),
                                     gmlp_norm_g[layer], w_spatial[layer], b_spatial[layer])
        q = apply_partial_rope(q.reshape(b, s, N_ATTN_HEADS, HEAD_DIM), cos, sin)
        k = apply_partial_rope(k.reshape(b, s, N_ATTN_HEADS, HEAD_DIM), cos, sin)
        v = v.reshape(b, s, N_ATTN_HEADS, HEAD_DIM)
        y_b = dilated_mixture_attention(q, k, v)
        gates = jax.nn.sigmoid(gate_logits.reshape(b, s, N_BRANCHES, D_MODEL))
        merged = gates[:, :, 0] * (y_a @ w_branch_a[layer]) + gates[:, :, 1] * (y_b @ w_branch_b[layer])
        x = x + merged @ w_out[layer]
        h2 = rms_norm(x, ffn_norm_g[layer])
        up = h2 @ w_up[layer]
        a, val = up[..., :D_FF_2], up[..., D_FF_2:]
        a = causal_depthwise_conv(a, conv_w[layer], conv_b[layer])
        x = x + (jax.nn.gelu(a, approximate=False) * val) @ w_down[layer]
    return rms_norm(x, final_norm_g)


def setup_inputs(seed=0):
    out = dict(first_inputs(seed))
    for name, value in second_inputs(seed + 1).items():
        if name != "x":
            out[name + "_2"] = value
    return out


def reference(
    x, c, ada_w, ada_b, norm1_g, norm2_g, a_w_qkv, a_w_o, a_lam_q1, a_lam_k1, a_lam_q2,
    a_lam_k2, a_subln_g, b_w_qkv, b_w_o, b_qnorm_g, b_knorm_g, f_w_in, f_w_out, final_g,
    positions_2, mix_norm_g_2, w_in_2, gmlp_norm_g_2, w_spatial_2, b_spatial_2, w_branch_a_2,
    w_branch_b_2, w_out_2, ffn_norm_g_2, w_up_2, conv_w_2, conv_b_2, w_down_2, final_norm_g_2,
):
    x = first_block(
        x, c, ada_w, ada_b, norm1_g, norm2_g, a_w_qkv, a_w_o, a_lam_q1, a_lam_k1, a_lam_q2,
        a_lam_k2, a_subln_g, b_w_qkv, b_w_o, b_qnorm_g, b_knorm_g, f_w_in, f_w_out, final_g,
    )
    return second_block(
        x, positions_2, mix_norm_g_2, w_in_2, gmlp_norm_g_2, w_spatial_2, b_spatial_2,
        w_branch_a_2, w_branch_b_2, w_out_2, ffn_norm_g_2, w_up_2, conv_w_2, conv_b_2, w_down_2,
        final_norm_g_2,
    )


_drawn_inputs = setup_inputs


def setup_inputs(seed=0):
    import zlib

    import numpy as np

    out = dict(_drawn_inputs(seed))
    spreads = {}
    factors = {'ada_b': 2.785,
     'norm1_g': 8.0,
     'norm2_g': 5.829,
     'a_lam_q1': 3.585,
     'a_lam_k1': 8.0,
     'a_lam_q2': 8.0,
     'a_subln_g': 8.0,
     'b_qnorm_g': 8.0,
     'b_knorm_g': 8.0,
     'mix_norm_g_2': 4.736,
     'gmlp_norm_g_2': 8.0,
     'ffn_norm_g_2': 10.926,
     'conv_b_2': 31.464,
     'final_norm_g_2': 8.064}
    for name, (base, spread) in spreads.items():
        noise = np.random.default_rng([zlib.crc32(name.encode()), seed]).standard_normal(out[name].shape)
        drawn = base * np.exp(spread * noise) if base else spread * noise
        out[name] = __import__('jax').numpy.asarray(drawn.astype(out[name].dtype))
    for name, factor in factors.items():
        out[name] = (out[name] * factor).astype(out[name].dtype)
    return out
```

```python
import math
from contextlib import ExitStack

import numpy as np

import concourse.bass as bass
from concourse import mybir

F32 = mybir.dt.float32
F32R = mybir.dt.float32r
I32 = mybir.dt.int32
ALU = mybir.AluOpType
ACT = mybir.ActivationFunctionType
AX = mybir.AxisListType

P = 128
D = 1024
S = 256
T = S // P
KD = D // P
FF = 2816
KF = FF // P
CH = 512
HC = CH // 2
NCH_FF = FF // HC
EPS = 1e-6
SIDE = 8
VECS = 11
W2_COLS = 5888
LAM_INIT = 0.8 - 0.6 * math.exp(-0.3 * 0)
TWO_PI = 2 * math.pi
ROUND = 1.5 * 2.0 ** 23

QKV_A, WO_A, IN_0, OUT_0, QKV_B, WO_B, IN_1, OUT_1 = 0, 24, 32, 76, 98, 110, 118, 162
IN_C, TAIL_C, BR_A, BR_B, OUT_C, UP_C, DOWN_C, END = 184, 228, 230, 236, 238, 246, 290, 312
RAW = 8
SPL = 4
LOOP = 8

ADA_SLOTS = 4
ADA_AT = (1, 1, 2, 1, 1, 2, 0, 0)
ADA_BEFORE = (0, 1, 2, 4, 5, 6, 8, 8)
GROUPS = 24


def at(const, turn=None, per=0):
    return const if turn is None else const + turn * per


def cols(start, turn, per, size):
    return slice(start, start + size) if turn is None else bass.ds(turn * per + start, size)


def program(nc, x_in, c_in, ada_w, ada_b, norm1_g, norm2_g, a_w_qkv, a_w_o, lq1, lk1, lq2, lk2,
            subln_g, b_w_qkv, b_w_o, qnorm_g, knorm_g, f_w_in, f_w_out, final_g, positions,
            mix_g, w_in_c, gmlp_g, w_spatial, b_spatial, w_branch_a, w_branch_b, w_out_c, ffn_g_c,
            w_up_c, conv_w, conv_b, w_down_c, final_g_c, rope_a, rope_b, inv_freq, masks, out,
            stop=99):
    ctx = ExitStack()
    with ctx:
        def sem(name):
            return ctx.enter_context(nc.semaphore(name))

        def sb(name, shape, dt=F32):
            return ctx.enter_context(nc.sbuf_tensor(name, shape, dt))

        raw = sb("raw", [P, RAW, 2, CH])
        ada = sb("ada", [P, ADA_SLOTS, 2, CH])
        w_hi = sb("w_hi", [P, SPL, 2, CH], F32R)
        w_lo = sb("w_lo", [P, SPL, 2, CH], F32R)
        h_hi = sb("h_hi", [P, KD, S], F32R)
        h_lo = sb("h_lo", [P, KD, S], F32R)
        x = sb("x", [P, T, D])
        ident = sb("ident", [P, P])
        ones = sb("ones", [P, P])
        vecs = sb("vecs", [P, 237])
        cond = sb("cond", [P, KD])
        half = sb("half", [P, 20])
        mod = sb("mod", [P, 4 * GROUPS])
        gains = sb("gains", [P, KD])
        stat = sb("stat", [P, 176])
        ada_acc = sb("ada_acc", [P, 2, CH])
        gate_row = sb("gate_row", [P, D])
        rope_a_sb = sb("rope_a_sb", [P, T, 2, 16])
        rope_c_sb = sb("rope_c_sb", [P, T, 2, 16])
        w_spT = sb("w_spT", [P, 4, P])
        REG_U = 2 * KF * S * 4
        REG_P = T * W2_COLS * 4
        u_base = nc.sbuf_base
        u_base = (u_base + 63) // 64 * 64
        p_base = u_base + REG_U
        arena = sb("arena", [P, (REG_U + REG_P) // 4 + 16])

        def at_u(name, shape, first, dt=F32):
            return nc.alloc_sbuf_tensor_at(name, shape, dt, offset=u_base + 4 * first)

        def at_p(name, shape, first, dt=F32):
            return nc.alloc_sbuf_tensor_at(name, shape, dt, offset=p_base + 4 * first)

        u_hi = at_u("u_hi", [P, KF, S], 0, F32R)
        u_lo = at_u("u_lo", [P, KF, S], KF * S, F32R)
        qkT = at_u("qkT", [P, 16, S], 0)
        prob_a = at_u("prob_a", [P, 2, 2, T, S], 4096)
        rope_t = at_u("rope_t", [P, T, 32, 16], 4096)
        wgt = at_u("wgt", [P, 2, T, S], 6144)
        wgtT = at_u("wgtT", [P, 2, T, S], 7168)
        att = at_u("att", [P, T, D], 8192)
        swap_b = at_u("swap_b", [P, T, 10, P], 2560)
        prob_b = at_u("prob_b", [P, 2, T, S], 5120)
        probT_b = at_u("probT_b", [P, 2, T, S], 6144)
        rope_b_sb = at_u("rope_b_sb", [P, T, 2, P], 7168)
        gain_b = at_u("gain_b", [P, 2, P], 7680)
        table_b = at_u("table_b", [P, T, 2, 2, P], 7936)
        att_b = at_u("att_b", [P, T, D], 8960)
        mask_sb = at_u("mask_sb", [P, 1152], 3072)
        prob_c = at_u("prob_c", [P, 2, 1152], 4224)
        probT_c = at_u("probT_c", [P, 9, P], 6528)
        y_c = at_u("y_c", [P, T, D], 7680)
        gmlp_row = at_u("gmlp_row", [P, 768], 9728)
        rope_tc = at_u("rope_tc", [P, T, 24, 16], 10496)
        proj = at_p("proj", [P, T, W2_COLS], 0)
        xn = at_p("xn", [P, T, D], 0)
        hf = at_p("hf", [P, KD, S], 2048)
        res = at_p("res", [P, 2 * T, CH], 4096)
        act_s = at_p("act_s", [P, 2, T, HC], 6144)
        act_u = at_p("act_u", [P, 2, T, HC], 7168)
        av = at_p("av", [P, 2, T, CH], 6144)
        conv_t = at_p("conv_t", [P, 2, 2, S], 8192)
        row = at_p("row", [P, D], 9216)
        diag = at_p("diag", [P, 4, P], 10240)
        stage_v = at_p("stage_v", [P, 3, P], 10752)
        lam_v = at_p("lam_v", [P, 4, 64], 11136)
        w_sp = at_p("w_sp", [P, 4, P], 9216)
        freq_row = at_p("freq_row", [P, 8], 11392)
        pos_i = at_p("pos_i", [P, T], 11400, I32)
        pos_f = at_p("pos_f", [P, T], 11408)
        ang = at_p("ang", [P, T, 8], 11416)
        ang_n = at_p("ang_n", [P, T, 2, 8], 11432)
        ang_r = at_p("ang_r", [P, T, 2, 8], 11464)
        c_rows = at_p("c_rows", [KD, P], 11504)
        merged = at_p("merged", [P, T, D], 0)
        merged_b = at_p("merged_b", [P, 2 * T, CH], W2_COLS)

        bank = [ctx.enter_context(nc.psum_tensor(f"bank{n}", [P, CH], F32)) for n in range(8)]

        N1_V, N2_V, MIX_V, FFN_V, SUB_V, BSP_V, CONV_V, ADAB_V = 0, 16, 32, 40, 48, 49, 53, 141
        SS, RSTD, MX, NMX, DEN, RDEN, MISC = 0, 20, 40, 72, 104, 136, 168
        neg_lam = stat[:, MISC:MISC + 1]

        raw_in = [sem(f"raw_in{n}") for n in range(RAW)]
        ada_in = [sem(f"ada_in{n}") for n in range(ADA_SLOTS)]
        hi_done = sem("hi_done")
        lo_done = sem("lo_done")
        mm_done = sem("mm_done")
        ada_done = sem("ada_done")
        ada_red = sem("ada_red")
        ada_col = sem("ada_col")
        c_load = sem("c_load")
        vec_in = sem("vec_in")
        side_in = sem("side_in")
        x_load = sem("x_load")
        late_in = [sem(f"late_in{n}") for n in range(4)]
        const_ok = sem("const_ok")
        setup = sem("setup")
        setup_v = sem("setup_v")
        setup_t = sem("setup_t")
        setup_p = sem("setup_p")
        dve = sem("dve")
        dve_conv = sem("dve_conv")
        sq0, sq1 = sem("sq0"), sem("sq1")
        rstd_ok = sem("rstd_ok")
        xn0, xn1 = sem("xn0"), sem("xn1")
        pre_tmp = sem("pre_tmp")
        t_done = sem("t_done")
        hf_dve, hf_act = sem("hf_dve"), sem("hf_act")
        h_hi_ok, h_lo_ok = sem("h_hi_ok"), sem("h_lo_ok")
        x_ok = sem("x_ok")
        evac = sem("evac")
        gate_diag, gate_mm, gate_ok = sem("gate_diag"), sem("gate_mm"), sem("gate_ok")
        s_act = sem("s_act")
        u_ok = sem("u_ok")
        u_t = sem("u_t")
        u_hi_ok, u_lo_ok = sem("u_hi_ok"), sem("u_lo_ok")
        av_ok, av_t, conv_ok, gelu_ok, cu_ok, c_hi, c_lo = (
            sem(n) for n in ("av_ok", "av_t", "conv_ok", "gelu_ok", "cu_ok", "c_hi", "c_lo"))
        rope_ok = sem("rope_ok")
        qk_t = sem("qk_t")
        qk_d, qk_a = sem("qk_d"), sem("qk_a")
        sc_ok, nmx_ok, exp_ok, wgt_ok, wgt_t, wgt_ev, pv_ok, o_sq, o_ok = (
            sem(n) for n in ("sc_ok", "nmx_ok", "exp_ok", "wgt_ok", "wgt_t", "wgt_ev", "pv_ok", "o_sq", "o_ok"))
        qk_sq, qk_r = sem("qk_sq"), sem("qk_r")
        gm_sq, gm_r, gm_v, gm_mm, gm_y = (sem(n) for n in ("gm_sq", "gm_r", "gm_v", "gm_mm", "gm_y"))
        c_qkt, c_qkd, c_qka, c_sc, c_sm, c_exp, c_pt, c_pev, c_pv, c_o = (
            sem(n) for n in ("c_qkt", "c_qkd", "c_qka", "c_sc", "c_sm", "c_exp", "c_pt", "c_pev", "c_pv", "c_o"))
        gelu_z, sig_g, br_ok = sem("gelu_z"), sem("sig_g"), sem("br_ok")
        out_ok = sem("out_ok")
        stored = sem("stored")

        block = ctx.enter_context(nc.Block())

        @block.sync
        def _(sp):
            def slot_free(m, turn=None):
                if m >= RAW:
                    sp.wait_ge(lo_done, at(m - RAW + 1, turn, LOOP))

            def load_wide(m, w, u, c0, turn=None, n=CH, per=2 * CH):
                slot_free(m, turn)
                src = w.rearrange("(k p) n -> p k n", p=P)[:, 2 * u:2 * u + 2, cols(c0, turn, per, n)]
                sp.dma_start(raw[:, m % RAW], src).then_inc(raw_in[m % RAW], 32)

            def load_pair(m, w, u, c0, turn=None):
                slot_free(m, turn)
                v = w.rearrange("(k p) n -> p k n", p=P)
                for half in range(2):
                    src = v[:, 2 * u:2 * u + 2, cols(half * FF + c0, turn, CH, HC)]
                    sp.dma_start(raw[:, m % RAW, :, half * HC:(half + 1) * HC], src).then_inc(raw_in[m % RAW], 16)

            def load_tall(m, w, k):
                slot_free(m)
                sp.dma_start(raw[:, m % RAW], w[k * P:(k + 1) * P, :].rearrange("p (a n) -> p a n", a=2)).then_inc(
                    raw_in[m % RAW], 32)

            def load_ada(a, turn=None):
                g, u = divmod(a, 4)
                layer, g = divmod(g, 12)
                if a >= ADA_SLOTS:
                    sp.wait_ge(ada_done, at(2 * (a - ADA_SLOTS + 1), turn, 16))
                src = ada_w[layer].rearrange("(k p) n -> p k n", p=P)[:, 2 * u:2 * u + 2, cols(g * CH, turn, 2 * CH, CH)]
                sp.dma_start(ada[:, a % ADA_SLOTS], src).then_inc(ada_in[a % ADA_SLOTS], 16)

            def load_ada_step(base, j, turn=None):
                for n in range(ADA_AT[j]):
                    load_ada(base + ADA_BEFORE[j] + n, turn)

            sp.dma_start(c_rows[:], c_in[0].rearrange("(k p) -> k p", p=P)).then_inc(c_load, 16)
            for t in range(T):
                sp.dma_start(x[:, t], x_in[0, t * P:(t + 1) * P, :]).then_inc(x_load, 16)
            for a in range(16):
                load_ada(a)
            if stop < 1:
                return
            for m in range(8):
                load_wide(m, a_w_qkv[0], m % 4, m // 4 * CH)
            with sp.Fori(0, 2) as turn:
                for j in range(LOOP):
                    load_ada_step(16, j, turn)
                    load_wide(8 + j, a_w_qkv[0], j % 4, 2 * CH + j // 4 * CH, turn)
            for j in range(8):
                load_ada_step(32, j)
                load_tall(WO_A + j, a_w_o[0], j)
            for m in range(4):
                load_pair(IN_0 + m, f_w_in[0], m, 0)
            for m in range(8):
                load_pair(IN_0 + 4 + m, f_w_in[0], m % 4, (1 + m // 4) * HC)
            for j in range(8):
                load_ada_step(40, j)
                load_pair(IN_0 + 12 + j, f_w_in[0], j % 4, (3 + j // 4) * HC)
            with sp.Fori(0, 3) as turn:
                for j in range(LOOP):
                    load_ada_step(48, j, turn)
                    load_pair(IN_0 + 20 + j, f_w_in[0], j % 4, (5 + j // 4) * HC, turn)
            for j in range(8):
                load_ada_step(72, j)
                load_tall(OUT_0 + j, f_w_out[0], j)
            for k in range(8, KF):
                if k < 16:
                    load_ada_step(80, k - 8)
                else:
                    load_ada_step(88, k - 16)
                load_tall(OUT_0 + k, f_w_out[0], k)
            for m in range(12):
                load_wide(QKV_B + m, b_w_qkv[0], m % 4, m // 4 * CH)
            for k in range(KD):
                load_tall(WO_B + k, b_w_o[0], k)
            for m in range(4):
                load_pair(IN_1 + m, f_w_in[1], m, 0)
            with sp.Fori(0, 5) as turn:
                for j in range(LOOP):
                    load_pair(IN_1 + 4 + j, f_w_in[1], j % 4, (1 + j // 4) * HC, turn)
            for k in range(KF):
                load_tall(OUT_1 + k, f_w_out[1], k)
            with sp.Fori(0, 5) as turn:
                for j in range(LOOP):
                    load_wide(IN_C + j, w_in_c[0], j % 4, j // 4 * CH, turn)
            for j in range(4):
                load_wide(IN_C + 40 + j, w_in_c[0], j, 10 * CH)
            for j in range(2):
                slot_free(TAIL_C + j)
                src = w_in_c[0].rearrange("(k p) n -> p k n", p=P)[:, 4 * j:4 * j + 4, 11 * CH:W2_COLS]
                sp.dma_start(raw[:, (TAIL_C + j) % RAW].rearrange("p a (b n) -> p (a b) n", b=2), src).then_inc(
                    raw_in[(TAIL_C + j) % RAW], 32)
            for k in range(6):
                load_tall(BR_A + k, w_branch_a[0], k)
            for k in range(2):
                load_tall(BR_B + k, w_branch_b[0], k)
            for k in range(KD):
                load_tall(OUT_C + k, w_out_c[0], k)
            for m in range(4):
                load_pair(UP_C + m, w_up_c[0], m, 0)
            with sp.Fori(0, 5) as turn:
                for j in range(LOOP):
                    load_pair(UP_C + 4 + j, w_up_c[0], j % 4, (1 + j // 4) * HC, turn)
            for k in range(KF):
                load_tall(DOWN_C + k, w_down_c[0], k)
            for t in range(T):
                sp.wait_ge(out_ok, t + 1)
                sp.dma_start(out[0, t * P:(t + 1) * P, :], x[:, t]).then_inc(stored, 16)
            sp.wait_ge(stored, 16 * T)

        @block.gpsimd
        def _(pool):
            side = [pool.dma_start(w_sp[:], w_spatial[0].rearrange("g t s -> t g s"))]
            side += [pool.dma_start(lam_v[:, n, :], v[0].partition_broadcast(P)) for n, v in enumerate((lq1, lk1, lq2, lk2))]
            side += [pool.dma_start(freq_row[:], inv_freq.partition_broadcast(P))]
            with nc.allow_non_contiguous_dma(reason="256 positions"):
                side += [pool.dma_start(pos_i[:], positions[0].rearrange("(t p) -> p t", p=P))]
            side += [pool.dma_start(rope_a_sb[:], rope_a.rearrange("(t p) a r -> p t a r", p=P))]
            for load in side:
                load.then_inc(side_in, 16)
            nc.gpsimd.memset(ident[:], 0.0).then_inc(const_ok, 1)
            nc.gpsimd.memset(ones[:], 1.0).then_inc(const_ok, 1)
            nc.gpsimd.memset(half[:], -0.5).then_inc(const_ok, 1)
            pool.wait_ge(const_ok, 3)
            nc.gpsimd.affine_select(out=ident[:], in_=ident[:], compare_op=ALU.not_equal, fill=1.0, base=0,
                                    pattern=[[-1, P]], channel_multiplier=1).then_inc(const_ok, 1)
            pool.wait_ge(side_in, 16 * SIDE)
            nc.gpsimd.affine_select(out=w_sp[:], in_=w_sp[:], compare_op=ALU.is_ge, fill=0.0, base=0,
                                    pattern=[[0, 4], [-1, P]], channel_multiplier=1).then_inc(setup_p, 1)

            power = [0]

            def inv_sqrt(first, n, width):
                nc.gpsimd.tensor_scalar(stat[:, RSTD + first:RSTD + first + n], stat[:, SS + first:SS + first + n],
                                        1.0 / width, EPS, ALU.mult, ALU.add).then_inc(pre_tmp, 1)
                power[0] += 1
                pool.wait_ge(pre_tmp, power[0])
                return nc.gpsimd.tensor_tensor(stat[:, RSTD + first:RSTD + first + n],
                                               stat[:, RSTD + first:RSTD + first + n],
                                               half[:, 0:n], ALU.pow)

            def norm(v):
                pool.wait_ge(sq0, v + 1)
                pool.wait_ge(sq1, v + 1)
                inv_sqrt(0, 2, D).then_inc(rstd_ok, 1)

            norm(0)
            if stop < 3:
                return
            pool.wait_ge(o_sq, 8)
            inv_sqrt(0, 16, P).then_inc(qk_r, 1)
            norm(1)
            pool.wait_ge(mm_done, QKV_B)
            pool.dma_start(rope_b_sb[:], rope_b.rearrange("(t p) a d -> p t a d", p=P)).then_inc(late_in[0], 16)
            pool.dma_start(gain_b[:, 0, :], qnorm_g[0].partition_broadcast(P)).then_inc(late_in[0], 16)
            pool.dma_start(gain_b[:, 1, :], knorm_g[0].partition_broadcast(P)).then_inc(late_in[0], 16)
            norm(2)
            if stop < 6:
                return
            pool.wait_ge(qk_sq, 2)
            inv_sqrt(0, 20, P).then_inc(qk_r, 1)
            norm(3)
            if stop < 8:
                return
            pool.wait_ge(t_done, 4 * 6)
            pool.dma_start(row[:], final_g.partition_broadcast(P)).then_inc(late_in[1], 16)
            pool.wait_ge(mm_done, IN_C)
            pool.dma_start(mask_sb[:], masks).then_inc(late_in[2], 16)
            pool.dma_start(gmlp_row[:], gmlp_g[0].partition_broadcast(P)).then_inc(late_in[2], 16)
            norm(4)
            norm(5)
            if stop < 10:
                return
            pool.wait_ge(gm_sq, 1)
            inv_sqrt(0, 2, 768).then_inc(gm_r, 1)
            norm(6)
            pool.wait_ge(t_done, 4 * 10)
            pool.dma_start(row[:], final_g_c.partition_broadcast(P)).then_inc(late_in[3], 16)
            norm(7)

        AFFINE = {0: 0, 2: 1, 3: 2, 5: 3, 6: 4, 9: 5}

        @block.scalar
        def _(act):
            def split(m, turn=None):
                if m >= END:
                    return
                act.wait_ge(raw_in[m % RAW], at(32 * (m // RAW + 1), turn, 32))
                if m >= SPL:
                    act.wait_ge(mm_done, at(m - SPL + 1, turn, LOOP))
                nc.scalar.activation(w_hi[:, m % SPL], raw[:, m % RAW], ACT.Copy).then_inc(hi_done, 1)

            def square_1(n):
                if n == 0:
                    act.wait_ge(x_load, 16 * T)
                else:
                    act.wait_ge(x_ok, 2 * n)
                nc.scalar.activation(xn[:, 1], x[:, 1], ACT.Square, accum_out=stat[:, SS + 1:SS + 2]).then_inc(sq1, 1)

            def scale_1(n):
                act.wait_ge(rstd_ok, n + 1)
                nc.scalar.activation(xn[:, 1], x[:, 1], ACT.Copy, scale=stat[:, RSTD + 1:RSTD + 2]).then_inc(xn1, 1)

            def operand(v, gain=None, shift=None, column=None):
                def affine(kk):
                    act.wait_ge(t_done, 4 * v + kk + 1)
                    for k in (2 * kk, 2 * kk + 1):
                        last = nc.scalar.activation(
                            hf[:, k], bank[4 + kk][:, k % 2 * S:(k % 2 + 1) * S], ACT.Identity, scale=gain[:, k:k + 1],
                            bias=0.0 if shift is None else shift[:, k:k + 1])
                    last.then_inc(hf_act, 1)

                for kk in range(4):
                    if v in AFFINE:
                        if kk in (0, 2):
                            affine(kk + 1)
                            act.wait_ge(hf_dve, 2 * AFFINE[v] + kk // 2 + 1)
                        else:
                            act.wait_ge(hf_act, 2 * AFFINE[v] + kk // 2 + 1)
                        nc.scalar.activation(h_hi[:, 2 * kk:2 * kk + 2], hf[:, 2 * kk:2 * kk + 2], ACT.Copy).then_inc(h_hi_ok, 1)
                    else:
                        act.wait_ge(t_done, 4 * v + kk + 1)
                        nc.scalar.activation(h_hi[:, 2 * kk:2 * kk + 2], bank[4 + kk][:].rearrange("p (k s) -> p k s", k=2),
                                             ACT.Copy, scale=1.0 if column is None else column).then_inc(h_hi_ok, 1)

            def take_chunk(base, done, c, b, turn=None):
                act.wait_ge(mm_done, at(base + 4 * (c + 1), turn, LOOP))
                for t in range(T):
                    last = nc.scalar.activation(proj[:, t, cols(c * CH, turn, 2 * CH, CH)], bank[2 * b + t][:], ACT.Copy)
                last.then_inc(evac, 1)

            def gate(n):
                for h in range(2):
                    act.wait_ge(gate_mm, 2 * n + h + 1)
                    nc.scalar.activation(gate_row[:, h * CH:(h + 1) * CH], bank[7][:], ACT.Copy).then_inc(gate_ok, 1)

            for n, (src, first, rows, group) in enumerate((
                    (norm1_g[0], 0, 8, 0), (norm1_g[1], 8, 8, 0), (norm2_g[0], 16, 8, 0), (norm2_g[1], 24, 8, 0),
                    (mix_g[0], 32, 8, 0), (ffn_g_c[0], 40, 8, 0), (subln_g[0], 48, 1, 0))):
                act.dma_start(stage_v[first:first + rows, group, :], src.rearrange("(k p) -> k p", p=P)).then_inc(vec_in, 16)
            act.dma_start(stage_v[49:53, 0, :], b_spatial[0]).then_inc(vec_in, 16)
            act.dma_start(stage_v[0:96, 2, :], ada_b.rearrange("l (k p) -> (l k) p", p=P)).then_inc(vec_in, 16)
            act.dma_start(stage_v[0:3 * KF, 1, :], conv_w[0].rearrange("j (k p) -> (j k) p", p=P)).then_inc(vec_in, 16)
            act.dma_start(stage_v[3 * KF:4 * KF, 1, :], conv_b[0].rearrange("(k p) -> k p", p=P)).then_inc(vec_in, 16)
            act.wait_ge(setup_t, 1)
            nc.scalar.activation(cond[:], bank[5][:, 0:KD], ACT.Silu).then_inc(setup, 1)
            square_1(0)
            act.wait_ge(setup_t, 2)
            nc.scalar.activation(vecs[:], bank[7][:, 0:237], ACT.Copy).then_inc(setup, 1)
            scale_1(0)
            act.wait_ge(setup_v, 1)
            nc.scalar.activation(stat[:, MISC + 4:MISC + 6], stat[:, MISC + 2:MISC + 4], ACT.Exp).then_inc(setup, 1)
            act.wait_ge(setup_t, 3)
            nc.scalar.activation(w_spT[:], bank[6][:].rearrange("p (g t) -> p g t", g=4), ACT.Copy).then_inc(setup, 1)
            act.wait_ge(setup_v, 2)
            nc.scalar.activation(ang_r[:], ang_r[:], ACT.Sin).then_inc(setup, 1)
            if stop < 1:
                return
            for m in range(SPL):
                split(m)
            operand(0, gains[:], mod[:, 0:8])
            with act.Fori(0, 3) as turn:
                for j in range(LOOP):
                    split(QKV_A + SPL + j, turn)
                    if j % 4 == 3:
                        take_chunk(QKV_A, 0, j // 4, j // 4, turn)
            gate(0)
            if stop < 2:
                return
            for n, f in enumerate((0, 4, 1, 5, 2, 6, 3, 7)):
                if n % 2:
                    act.wait_ge(qk_t, n + 1)
                    nc.scalar.activation(qkT[:, 2 * f:2 * f + 2], bank[4 + n % 4][:].rearrange("p (k s) -> p k s", k=2),
                                         ACT.Copy).then_inc(qk_a, 1)
            NH = 8
            for i in range(NH + 2):
                if i < NH:
                    act.wait_ge(nmx_ok, i + 1)
                    for c in range(2):
                        for t in range(T):
                            n = 4 * i + 2 * c + t
                            last = nc.scalar.activation(
                                prob_a[:, i % 2, c, t], bank[2 * (i % 2) + c][:, t * S:(t + 1) * S], ACT.Exp,
                                bias=stat[:, NMX + n:NMX + n + 1], scale=0.125, accum_out=stat[:, DEN + n:DEN + n + 1])
                    last.then_inc(exp_ok, 1)
                if 1 <= i <= NH:
                    h = i - 1
                    act.wait_ge(wgt_t, h + 1)
                    nc.scalar.activation(wgtT[:, h % 2], bank[4 + h % 2][:].rearrange("p (k s) -> p k s", k=2),
                                         ACT.Copy).then_inc(wgt_ev, 1)
                if i >= 2:
                    h = i - 2
                    act.wait_ge(pv_ok, h + 1)
                    for t in range(T):
                        last = nc.scalar.activation(att[:, t, h * P:(h + 1) * P], bank[6 + h % 2][:, t * P:(t + 1) * P],
                                                    ACT.Square, accum_out=stat[:, SS + 2 * h + t:SS + 2 * h + t + 1])
                    last.then_inc(o_sq, 1)
            operand(1, column=stat[:, MISC + 6:MISC + 7])
            for m in range(WO_A, IN_0):
                split(m + SPL)
            if stop < 3:
                return
            square_1(1)
            scale_1(1)
            operand(2, gains[:], mod[:, 24:32])

            def silu(base, f, c, b, turn=None):
                act.wait_ge(mm_done, at(base + 4 * (c + 1), turn, LOOP))
                for t in range(T):
                    last = nc.scalar.activation(act_s[:, b, t], bank[2 * b + t][:, 0:HC], ACT.Silu)
                last.then_inc(s_act, 1)

            def u_high(f, c, b, turn=None):
                act.wait_ge(u_t, at(NCH_FF * f + c + 1, turn, 2))
                nc.scalar.activation(u_hi[:, cols(2 * c, turn, 4, 2), :], bank[4 + b][:].rearrange("p (k s) -> p k s", k=2),
                                     ACT.Copy).then_inc(u_hi_ok, 1)

            def feed_forward(base, f, gate_n):
                for j in range(4):
                    split(base + SPL + j)
                silu(base, f, 0, 0)
                with act.Fori(0, 5) as turn:
                    for j in range(LOOP):
                        if j % 4 == 3:
                            u_high(f, j // 4, j // 4, turn)
                        split(base + 4 + SPL + j, turn)
                        if j % 4 == 3:
                            silu(base, f, 1 + j // 4, 1 - j // 4, turn)
                for k in range(KF):
                    if k == 3:
                        u_high(f, NCH_FF - 1, 0)
                    split(base + 4 * NCH_FF + SPL + k)
                    if k == 6:
                        gate(gate_n)

            feed_forward(IN_0, 0, 1)
            if stop < 4:
                return
            square_1(2)
            scale_1(2)
            operand(3, gains[:], mod[:, 48:56])
            for j in range(12):
                split(QKV_B + SPL + j)
                if j % 4 == 3:
                    take_chunk(QKV_B, 6, j // 4, j // 4 % 2)
            gate(2)
            if stop < 5:
                return
            act.wait_ge(evac, 9)
            for h in range(10):
                last = nc.scalar.activation(swap_b[:, 1, h], proj[:, 1, h * P:(h + 1) * P], ACT.Square,
                                            accum_out=stat[:, SS + 2 * h + 1:SS + 2 * h + 2])
            last.then_inc(qk_sq, 1)
            for f in range(5):
                if f % 2:
                    act.wait_ge(qk_t, 8 + f + 1)
                    nc.scalar.activation(qkT[:, 2 * f:2 * f + 2], bank[4 + f % 4][:].rearrange("p (k s) -> p k s", k=2),
                                         ACT.Copy).then_inc(qk_a, 1)
            for i in range(NH + 1):
                if i < NH:
                    act.wait_ge(nmx_ok, 8 + i + 1)
                    for t in range(T):
                        n = 2 * i + t
                        last = nc.scalar.activation(prob_b[:, i % 2, t], bank[i % 4][:, t * S:(t + 1) * S], ACT.Exp,
                                                    bias=stat[:, NMX + n:NMX + n + 1], scale=stat[:, RDEN + n:RDEN + n + 1],
                                                    accum_out=stat[:, DEN + n:DEN + n + 1])
                    last.then_inc(exp_ok, 1)
                if i >= 1:
                    h = i - 1
                    act.wait_ge(wgt_t, 8 + h + 1)
                    nc.scalar.activation(probT_b[:, h % 2], bank[4 + h % 2][:].rearrange("p (k s) -> p k s", k=2),
                                         ACT.Copy).then_inc(wgt_ev, 1)
            operand(4)
            for m in range(WO_B, IN_1):
                split(m + SPL)
            if stop < 6:
                return
            square_1(3)
            scale_1(3)
            operand(5, gains[:], mod[:, 72:80])
            feed_forward(IN_1, 1, 3)
            if stop < 7:
                return
            square_1(4)
            square_1(5)
            scale_1(5)
            operand(6, vecs[:, MIX_V:MIX_V + KD])
            with act.Fori(0, 2) as turn:
                for j in range(LOOP):
                    split(IN_C + SPL + j, turn)
                    if j % 4 == 3:
                        take_chunk(IN_C, 9, j // 4, j // 4, turn)
            act.wait_ge(evac, 9 + 4)
            for t in range(T):
                last = nc.scalar.activation(proj[:, t, 0:1536], proj[:, t, 0:1536], ACT.Gelu)
            last.then_inc(gelu_z, 1)
            act.wait_ge(gelu_z, 1)
            for t in range(T):
                last = nc.scalar.activation(rope_tc[:].rearrange("p a b c -> p (a b c)"), proj[:, t, 768:1536], ACT.Square,
                                            accum_out=stat[:, SS + t:SS + t + 1])
                if t == 0:
                    last.then_inc(gelu_z, 1)
                    act.wait_ge(gelu_z, 2)
            last.then_inc(gm_sq, 1)
            with act.Fori(0, 3) as turn:
                for j in range(LOOP):
                    split(IN_C + 16 + SPL + j, turn)
                    if j % 4 == 3:
                        act.wait_ge(mm_done, at(IN_C + 16 + 4 * (j // 4 + 1), turn, LOOP))
                        for t in range(T):
                            last = nc.scalar.activation(proj[:, t, cols((4 + j // 4) * CH, turn, 2 * CH, CH)],
                                                        bank[2 * (j // 4) + t][:], ACT.Copy)
                        last.then_inc(evac, 1)
            act.wait_ge(gm_r, 1)
            for t in range(T):
                last = nc.scalar.activation(proj[:, t, 768:1536], proj[:, t, 768:1536], ACT.Copy,
                                            scale=stat[:, RSTD + t:RSTD + t + 1])
            last.then_inc(gm_v, 1)
            for j in range(4):
                split(IN_C + 40 + SPL + j)
            take_chunk(IN_C, 9, 10, 0)
            for j in range(2):
                split(TAIL_C + SPL + j)
            act.wait_ge(mm_done, TAIL_C + 2)
            for t in range(T):
                last = nc.scalar.activation(proj[:, t, 11 * CH:W2_COLS], bank[2 + t][:, 0:HC], ACT.Copy)
            last.then_inc(evac, 1)
            if stop < 8:
                return
            for f in range(6):
                if f % 2:
                    act.wait_ge(c_qkt, f + 1)
                    nc.scalar.activation(qkT[:, 2 * f:2 * f + 2], bank[4 + f % 4][:].rearrange("p (k s) -> p k s", k=2),
                                         ACT.Copy).then_inc(c_qka, 1)
            for i in range(4):
                act.wait_ge(c_sm, i + 1)
                for t, (first, width) in enumerate(((0, 384), (384, 768))):
                    n = 2 * i + t
                    part = prob_c[:, i % 2, first:first + width]
                    last = nc.scalar.activation(part, part, ACT.Exp, bias=stat[:, NMX + n:NMX + n + 1],
                                                accum_out=stat[:, DEN + n:DEN + n + 1])
                last.then_inc(c_exp, 1)
                act.wait_ge(c_pt, i + 1)
                if i >= 1:
                    act.wait_ge(c_pv, i)
                for q, (first, n) in enumerate(((0, 4), (4, 4), (8, 1))):
                    last = nc.scalar.activation(probT_c[:, first:first + n], bank[3 + q][:, 0:n * P].rearrange(
                        "p (k s) -> p k s", k=n), ACT.Copy)
                last.then_inc(c_pev, 1)
            act.wait_ge(evac, 9 + 12)
            for t in range(T):
                last = nc.scalar.activation(proj[:, t, 3840:W2_COLS], proj[:, t, 3840:W2_COLS], ACT.Sigmoid)
            last.then_inc(sig_g, 1)
            operand(7)
            for m in range(BR_A, OUT_C):
                split(m + SPL)
            operand(8)
            for m in range(OUT_C, UP_C):
                split(m + SPL)
            if stop < 9:
                return
            square_1(6)
            scale_1(6)
            operand(9, vecs[:, FFN_V:FFN_V + KD])

            def take_pair(c, b, turn=None):
                act.wait_ge(mm_done, at(UP_C + 4 * (c + 1), turn, LOOP))
                for t in range(T):
                    last = nc.scalar.activation(av[:, b, t], bank[2 * b + t][:], ACT.Copy)
                last.then_inc(av_ok, 1)

            def gelu(c, b, turn=None):
                act.wait_ge(conv_ok, at(c + 1, turn, 2))
                nc.scalar.activation(conv_t[:, b], conv_t[:, b], ACT.Gelu).then_inc(gelu_ok, 1)

            def c_high(c, b, turn=None):
                act.wait_ge(cu_ok, at(c + 1, turn, 2))
                nc.scalar.activation(u_hi[:, cols(2 * c, turn, 4, 2), :], conv_t[:, b], ACT.Copy).then_inc(c_hi, 1)

            for j in range(4):
                split(UP_C + SPL + j)
            take_pair(0, 0)
            with act.Fori(0, 5) as turn:
                for j in range(LOOP):
                    split(UP_C + 4 + SPL + j, turn)
                    if j % 4 == 2:
                        gelu(j // 4, j // 4, turn)
                    if j % 4 == 3:
                        c_high(j // 4, j // 4, turn)
                        take_pair(1 + j // 4, 1 - j // 4, turn)
            for k in range(KF):
                split(DOWN_C + SPL + k)
                if k == 2:
                    gelu(NCH_FF - 1, 0)
                if k == 3:
                    c_high(NCH_FF - 1, 0)
            square_1(7)

        @block.vector
        def _(v_):
            ve = nc.vector
            chain = [0]

            def link(ins):
                chain[0] += 1
                ins.then_inc(dve, 1)
                v_.wait_ge(dve, chain[0])

            def low(m, turn=None):
                if m >= END:
                    return
                v_.wait_ge(hi_done, at(m + 1, turn, LOOP))
                ve.tensor_tensor(w_lo[:, m % SPL], raw[:, m % RAW], w_hi[:, m % SPL].bitcast(F32),
                                 ALU.subtract).then_inc(lo_done, 1)

            def fold(a, turn=None):
                g, u = divmod(a, 4)
                v_.wait_ge(ada_in[a % ADA_SLOTS], at(16 * (a // ADA_SLOTS + 1), turn, 32))
                for k in range(2):
                    n = 2 * a + k
                    w = ada[:, a % ADA_SLOTS, k]
                    if n % 8 == 0:
                        if g >= 2:
                            v_.wait_ge(ada_red, at(g - 1, turn, 2))
                        ve.tensor_scalar(ada_acc[:, g % 2], w, cond[:, 0:1], None, ALU.mult).then_inc(ada_done, 1)
                    else:
                        v_.wait_ge(ada_done, at(n, turn, 16))
                        ve.scalar_tensor_tensor(out=ada_acc[:, g % 2], in0=w, scalar=cond[:, n % 8:n % 8 + 1],
                                                in1=ada_acc[:, g % 2], op0=ALU.mult, op1=ALU.add).then_inc(ada_done, 1)

            def take_group(g, turn=None):
                v_.wait_ge(ada_red, at(g + 1, turn, 2))
                ve.tensor_tensor(mod[:, cols(4 * g, turn, 8, 4)], bank[6][:, 0:4],
                                 vecs[:, cols(ADAB_V + 4 * g, turn, 8, 4)], ALU.add).then_inc(ada_col, 1)

            def fold_step(base, j, turn=None):
                for n in range(ADA_AT[j]):
                    fold(base + ADA_BEFORE[j] + n, turn)
                if j == 6:
                    take_group(base // 4, turn)
                if j == 7:
                    take_group(base // 4 + 1, turn)

            def square_0(n):
                if n == 0:
                    v_.wait_ge(x_load, 16 * T)
                ve.tensor_tensor_reduce(out=xn[:, 0], in0=x[:, 0], in1=x[:, 0], scale=1.0, scalar=0.0, op0=ALU.mult,
                                        op1=ALU.add, accum_out=stat[:, SS:SS + 1]).then_inc(sq0, 1)

            def scale_0(n):
                v_.wait_ge(rstd_ok, n + 1)
                ve.tensor_scalar(xn[:, 0], x[:, 0], stat[:, RSTD:RSTD + 1], None, ALU.mult).then_inc(xn0, 1)

            def make_gains(first, group):
                v_.wait_ge(ada_col, group)
                link(ve.scalar_tensor_tensor(out=gains[:], in0=mod[:, 4 * (group - 2):4 * group], scalar=1.0,
                                             in1=vecs[:, first:first + KD], op0=ALU.add, op1=ALU.mult))

            def operand(v, gain=None, shift=None, column=None):
                if v in AFFINE:
                    for kk in (0, 2):
                        v_.wait_ge(t_done, 4 * v + kk + 1)
                        for k in (2 * kk, 2 * kk + 1):
                            last = ve.tensor_scalar(hf[:, k], bank[4 + kk][:, k % 2 * S:(k % 2 + 1) * S], gain[:, k:k + 1],
                                                    0.0 if shift is None else shift[:, k:k + 1], ALU.mult, ALU.add)
                        last.then_inc(hf_dve, 1)
                for kk in range(4):
                    v_.wait_ge(h_hi_ok, 4 * v + kk + 1)
                    out_, hi = h_lo[:, 2 * kk:2 * kk + 2], h_hi[:, 2 * kk:2 * kk + 2].bitcast(F32)
                    ps = bank[4 + kk][:].rearrange("p (k s) -> p k s", k=2)
                    if v in AFFINE:
                        last = ve.tensor_tensor(out_, hf[:, 2 * kk:2 * kk + 2], hi, ALU.subtract)
                    elif column is None:
                        last = ve.tensor_tensor(out_, ps, hi, ALU.subtract)
                    else:
                        last = ve.scalar_tensor_tensor(out=out_, in0=ps, scalar=column, in1=hi, op0=ALU.mult,
                                                       op1=ALU.subtract)
                    last.then_inc(h_lo_ok, 1)

            def gate(n, first, h):
                if 2 * n + h:
                    v_.wait_ge(gate_mm, 2 * n + h)
                c0 = first + 4 * h
                ve.tensor_tensor(diag[:], ident[:].unsqueeze(1).to_broadcast([P, 4, P]),
                                 mod[:, c0:c0 + 4].unsqueeze(2).to_broadcast([P, 4, P]), ALU.mult).then_inc(gate_diag, 1)

            def residual(done, gated):
                v_.wait_ge(mm_done, done)
                if gated is not None:
                    v_.wait_ge(gate_ok, 2 * gated + 2)
                    for t in range(T):
                        for n in range(2):
                            ve.tensor_tensor(res[:, 2 * t + n], bank[2 * n + t][:], gate_row[:, n * CH:(n + 1) * CH],
                                             ALU.mult)
                    link(ve.tensor_copy(stat[:, MISC + 7:MISC + 8], neg_lam))
                for t in range(T):
                    for n in range(2):
                        part = x[:, t, n * CH:(n + 1) * CH]
                        if gated is not None:
                            last = ve.tensor_tensor(part, part, res[:, 2 * t + n], ALU.add)
                        else:
                            last = ve.tensor_tensor(part, bank[2 * n + t][:], part, ALU.add)
                    last.then_inc(x_ok, 1)
                residuals[0] += 1
                v_.wait_ge(x_ok, 2 * residuals[0])

            residuals = [0]
            v_.wait_ge(setup, 1)
            square_0(0)
            for a in range(16):
                fold(a)
                if a == 1:
                    scale_0(0)
                if a % 4 == 1 and a > 4:
                    if a == 5:
                        v_.wait_ge(setup, 2)
                    take_group(a // 4 - 1)
            take_group(3)
            make_gains(N1_V, 4)
            def lam_and_angles():
                v_.wait_ge(side_in, 16 * SIDE)
                for n in range(2):
                    ins = ve.tensor_tensor_reduce(out=lam_v[:, 2 * n], in0=lam_v[:, 2 * n], in1=lam_v[:, 2 * n + 1], scale=1.0,
                                                  scalar=0.0, op0=ALU.mult, op1=ALU.add,
                                                  accum_out=stat[:, MISC + 2 + n:MISC + 3 + n])
                ins.then_inc(setup_v, 1)
                link(ve.tensor_copy(pos_f[:], pos_i[:]))
                link(ve.tensor_tensor(ang[:], pos_f[:].unsqueeze(2).to_broadcast([P, T, 8]),
                                      freq_row[:].unsqueeze(1).to_broadcast([P, T, 8]), ALU.mult))
                hi = 6.28125
                mid = float(np.float32(TWO_PI - hi)) // 2.0 ** -19 * 2.0 ** -19
                lo = TWO_PI - hi - mid
                for q, quarter in enumerate((math.pi / 2, 0.0)):
                    n, r = ang_n[:, :, q], ang_r[:, :, q]
                    link(ve.tensor_scalar(n, ang[:], 1 / TWO_PI, quarter / TWO_PI, ALU.mult, ALU.add))
                    link(ve.tensor_scalar(n, n, ROUND, None, ALU.add))
                    link(ve.tensor_scalar(n, n, ROUND, None, ALU.subtract))
                    link(ve.scalar_tensor_tensor(out=r, in0=n, scalar=-hi, in1=ang[:], op0=ALU.mult, op1=ALU.add))
                    link(ve.scalar_tensor_tensor(out=r, in0=n, scalar=-mid, in1=r, op0=ALU.mult, op1=ALU.add))
                    link(ve.scalar_tensor_tensor(out=r, in0=n, scalar=-lo, in1=r, op0=ALU.mult, op1=ALU.add))
                    link(ve.tensor_scalar(r, r, quarter, None, ALU.add))
                    link(ve.tensor_scalar(r, r, PI_IN, -PI_IN, ALU.min, ALU.max))
                ve.tensor_copy(stat[:, MISC + 7:MISC + 8], stat[:, MISC + 2:MISC + 3]).then_inc(setup_v, 1)
                v_.wait_ge(setup, 3)
                link(ve.tensor_tensor(neg_lam, stat[:, MISC + 5:MISC + 6], stat[:, MISC + 4:MISC + 5], ALU.subtract))
                link(ve.tensor_scalar(neg_lam, neg_lam, LAM_INIT, None, ALU.subtract))
                link(ve.tensor_scalar(stat[:, MISC + 6:MISC + 7], vecs[:, SUB_V:SUB_V + 1], 1.0 - LAM_INIT, None, ALU.mult))
                v_.wait_ge(setup, 5)
                for h in range(2):
                    ve.tensor_copy(rope_c_sb[:, :, 0, 8 * h:8 * h + 8], ang_r[:, :, 0])
                ve.tensor_scalar(rope_c_sb[:, :, 1, 0:8], ang_r[:, :, 1], -1.0, None, ALU.mult)
                link(ve.tensor_copy(rope_c_sb[:, :, 1, 8:16], ang_r[:, :, 1]))

            PI_IN = float(np.nextafter(np.float32(math.pi), np.float32(0)))
            lam_and_angles()
            if stop < 1:
                return
            operand(0, gains[:], mod[:, 0:8])
            for m in range(SPL):
                low(m)
            with v_.Fori(0, 3) as turn:
                for j in range(LOOP):
                    low(QKV_A + SPL + j, turn)
                    fold_step(16, j, turn)
            v_.wait_ge(ada_col, 10)
            for h in range(2):
                gate(0, 16, h)
            if stop < 2:
                return

            def rotate(first, heads, table, tmp, need):
                v_.wait_ge(evac, need)
                q = proj[:, :, first:first + heads * 64].rearrange("p t (h d) -> p t h d", d=64)[:, :, :, 0:16]
                for h in range(2):
                    for t in range(T):
                        last = ve.tensor_tensor(
                            tmp[:, t, :, 8 * h:8 * h + 8], q[:, t, :, 8 - 8 * h:16 - 8 * h],
                            table[:, t, 1, 8 * h:8 * h + 8].unsqueeze(1).to_broadcast([P, heads, 8]), ALU.mult)
                link(last)
                for t in range(T):
                    last = ve.tensor_tensor(q[:, t], q[:, t], table[:, t, 0].unsqueeze(1).to_broadcast([P, heads, 16]), ALU.mult)
                link(last)
                for t in range(T):
                    last = ve.tensor_tensor(q[:, t], q[:, t], tmp[:, t], ALU.add)
                last.then_inc(rope_ok, 1)

            rotate(0, 32, rope_a_sb, rope_t, 4)
            for n, f in enumerate((0, 4, 1, 5, 2, 6, 3, 7)):
                if n % 2 == 0:
                    v_.wait_ge(qk_t, n + 1)
                    ve.tensor_copy(qkT[:, 2 * f:2 * f + 2], bank[4 + n % 4][:].rearrange("p (k s) -> p k s", k=2)).then_inc(qk_d, 1)
            NH = 8
            for i in range(NH + 3):
                if i < NH:
                    v_.wait_ge(sc_ok, i + 1)
                    for c in range(2):
                        n = MX + 4 * i + 2 * c
                        last = ve.tensor_reduce(stat[:, n:n + 2], bank[2 * (i % 2) + c][:].rearrange("p (t s) -> p t s", t=2),
                                                AX.X, ALU.max)
                    link(last)
                    ve.tensor_scalar(stat[:, NMX + 4 * i:NMX + 4 * i + 4], stat[:, MX + 4 * i:MX + 4 * i + 4], -0.125, None,
                                     ALU.mult).then_inc(nmx_ok, 1)
                if 1 <= i <= NH:
                    h = i - 1
                    v_.wait_ge(exp_ok, h + 1)
                    r = stat[:, RDEN + 4 * h:RDEN + 4 * h + 4]
                    link(ve.reciprocal(r, stat[:, DEN + 4 * h:DEN + 4 * h + 4]))
                    link(ve.tensor_scalar(r[:, 2:4], r[:, 2:4], neg_lam, None, ALU.mult))
                    for t in range(T):
                        p1 = prob_a[:, h % 2, 1, t]
                        last = ve.tensor_scalar(p1, p1, r[:, 2 + t:3 + t], None, ALU.mult)
                    link(last)
                    if h >= 2:
                        v_.wait_ge(wgt_t, h - 1)
                    for t in range(T):
                        last = ve.scalar_tensor_tensor(out=wgt[:, h % 2, t], in0=prob_a[:, h % 2, 0, t], scalar=r[:, t:t + 1],
                                                       in1=prob_a[:, h % 2, 1, t], op0=ALU.mult, op1=ALU.add)
                    last.then_inc(wgt_ok, 1)
                if i >= 3:
                    h = i - 3
                    v_.wait_ge(o_sq, h + 1)
                    ve.tensor_copy(att[:, :, h * P:(h + 1) * P], bank[6 + h % 2][:, 0:2 * P].rearrange(
                        "p (t e) -> p t e", t=2)).then_inc(o_ok, 1)
            v_.wait_ge(qk_r, 1)
            v_.wait_ge(o_ok, 8)
            for t in range(T):
                o = att[:, t].rearrange("p (h e) -> p h e", e=P)
                r = stat[:, RSTD:RSTD + 16].rearrange("p (h t) -> p t h", t=2)[:, t]
                ve.tensor_tensor(o, o, r.unsqueeze(2).to_broadcast([P, 8, P]), ALU.mult).then_inc((xn0, xn1)[t], 1)
            operand(1, column=stat[:, MISC + 6:MISC + 7])
            for m in range(WO_A, IN_0):
                low(m + SPL)
            residual(IN_0, 0)
            if stop < 3:
                return
            square_0(1)
            make_gains(N2_V, 10)
            scale_0(1)
            operand(2, gains[:], mod[:, 24:32])

            def glu(f, c, b, turn=None):
                v_.wait_ge(s_act, at(NCH_FF * f + c + 1, turn, 2))
                for t in range(T):
                    last = ve.tensor_tensor(act_u[:, b, t], bank[2 * b + t][:, HC:CH], act_s[:, b, t], ALU.mult)
                last.then_inc(u_ok, 1)

            def u_low(f, c, b, turn=None):
                v_.wait_ge(u_hi_ok, at(NCH_FF * f + c + 1, turn, 2))
                ve.tensor_tensor(u_lo[:, cols(2 * c, turn, 4, 2), :], bank[4 + b][:].rearrange("p (k s) -> p k s", k=2),
                                 u_hi[:, cols(2 * c, turn, 4, 2), :].bitcast(F32), ALU.subtract).then_inc(u_lo_ok, 1)

            def feed_forward(base, f, gate_n, gate_c, with_ada):
                for j in range(4):
                    low(base + SPL + j)
                glu(f, 0, 0)
                with v_.Fori(0, 5) as turn:
                    for j in range(LOOP):
                        if j % 4 == 3:
                            u_low(f, j // 4, j // 4, turn)
                        low(base + 4 + SPL + j, turn)
                        if with_ada:
                            fold_step(40, j, turn)
                        if j % 4 == 3:
                            glu(f, 1 + j // 4, 1 - j // 4, turn)
                for k in range(KF):
                    if k == 3:
                        u_low(f, NCH_FF - 1, 0)
                    low(base + 4 * NCH_FF + SPL + k)
                    if with_ada and k < 16:
                        fold_step(80 + k // 8 * 8, k % 8)
                    if k == 4:
                        gate(gate_n, gate_c, 0)
                    if k == 5:
                        gate(gate_n, gate_c, 1)
                residual(base + 4 * NCH_FF + KF, gate_n)

            feed_forward(IN_0, 0, 1, 40, True)
            if stop < 4:
                return
            square_0(2)
            make_gains(N1_V + KD, 16)
            scale_0(2)
            operand(3, gains[:], mod[:, 48:56])
            for j in range(12):
                low(QKV_B + SPL + j)
            for h in range(2):
                gate(2, 64, h)
            if stop < 5:
                return

            v_.wait_ge(late_in[0], 48)
            for a in range(2):
                for t in range(T):
                    ve.tensor_tensor(table_b[:, t, a, 0], rope_b_sb[:, t, 0], gain_b[:, a], ALU.mult)
                    for lo, hi in ((0, 32), (32, 0), (64, 96), (96, 64)):
                        last = ve.tensor_tensor(table_b[:, t, a, 1, lo:lo + 32], rope_b_sb[:, t, 1, lo:lo + 32],
                                                gain_b[:, a, hi:hi + 32], ALU.mult)
            link(last)
            v_.wait_ge(evac, 9)
            link(ve.tensor_tensor(swap_b[:, 0], proj[:, 0, 0:1280].rearrange("p (h d) -> p h d", d=P),
                                  proj[:, 0, 0:1280].rearrange("p (h d) -> p h d", d=P), ALU.mult))
            ve.tensor_reduce(stat[:, SS:SS + 20].rearrange("p (h t) -> p t h", t=2)[:, 0], swap_b[:, 0], AX.X,
                             ALU.add).then_inc(qk_sq, 1)
            v_.wait_ge(qk_sq, 2)
            for t in range(T):
                for a, (h0, h1) in enumerate(((0, 8), (8, 10))):
                    q = proj[:, t, h0 * P:h1 * P].rearrange("p (h q e r) -> p h q e r", q=2, e=2, r=32)
                    sw = swap_b[:, t, h0:h1].rearrange("p h (q e r) -> p h q e r", q=2, e=2)
                    tab = table_b[:, t, a, 1].rearrange("p (q e r) -> p q e r", q=2, e=2)
                    for e in range(2):
                        for qq in range(2):
                            last = ve.tensor_tensor(sw[:, :, qq, e], q[:, :, qq, 1 - e],
                                                    tab[:, qq, e].unsqueeze(1).to_broadcast([P, h1 - h0, 32]), ALU.mult)
                link(last)
                for a, (h0, h1) in enumerate(((0, 8), (8, 10))):
                    q = proj[:, t, h0 * P:h1 * P].rearrange("p (h d) -> p h d", d=P)
                    last = ve.tensor_tensor(q, q, table_b[:, t, a, 0].unsqueeze(1).to_broadcast([P, h1 - h0, P]), ALU.mult)
                link(last)
                q = proj[:, t, 0:1280].rearrange("p (h d) -> p h d", d=P)
                last = ve.tensor_tensor(q, q, swap_b[:, t], ALU.add)
                link(last)
            v_.wait_ge(qk_r, 2)
            for t in range(T):
                k = proj[:, t, 1024:1280].rearrange("p (h d) -> p h d", d=P)
                r = stat[:, RSTD + 16:RSTD + 20].rearrange("p (h t) -> p t h", t=2)[:, t]
                last = ve.tensor_tensor(k, k, r.unsqueeze(2).to_broadcast([P, 2, P]), ALU.mult)
            last.then_inc(rope_ok, 1)
            link(ve.tensor_scalar(stat[:, RDEN:RDEN + 16], stat[:, RSTD:RSTD + 16], P ** -0.5, None, ALU.mult))
            for f in range(5):
                if f % 2 == 0:
                    v_.wait_ge(qk_t, 8 + f + 1)
                    ve.tensor_copy(qkT[:, 2 * f:2 * f + 2], bank[4 + f % 4][:].rearrange("p (k s) -> p k s", k=2)).then_inc(qk_d, 1)
            for i in range(NH + 2):
                if i < NH:
                    v_.wait_ge(sc_ok, 8 + i + 1)
                    n = MX + 2 * i
                    link(ve.tensor_reduce(stat[:, n:n + 2], bank[i % 4][:].rearrange("p (t s) -> p t s", t=2), AX.X, ALU.max))
                    ve.scalar_tensor_tensor(out=stat[:, NMX + 2 * i:NMX + 2 * i + 2], in0=stat[:, n:n + 2], scalar=-1.0,
                                            in1=stat[:, RDEN + 2 * i:RDEN + 2 * i + 2], op0=ALU.mult,
                                            op1=ALU.mult).then_inc(nmx_ok, 1)
                if i >= 2:
                    h = i - 2
                    v_.wait_ge(pv_ok, 8 + h + 1)
                    den = stat[:, DEN + 2 * h:DEN + 2 * h + 2]
                    link(ve.reciprocal(den, den))
                    for t in range(T):
                        last = ve.tensor_scalar(att_b[:, t, h * P:(h + 1) * P], bank[6 + h % 2][:, t * P:(t + 1) * P],
                                                den[:, t:t + 1], None, ALU.mult)
                        if h == NH - 1:
                            last.then_inc((xn0, xn1)[t], 1)
                    if h < NH - 1:
                        last.then_inc(o_ok, 1)
            operand(4)
            for m in range(WO_B, IN_1):
                low(m + SPL)
            residual(IN_1, 2)
            if stop < 6:
                return
            square_0(3)
            make_gains(N2_V + KD, 22)
            scale_0(3)
            operand(5, gains[:], mod[:, 72:80])
            feed_forward(IN_1, 1, 3, 88, False)
            if stop < 7:
                return
            square_0(4)
            v_.wait_ge(late_in[1], 16)
            v_.wait_ge(rstd_ok, 5)
            for t in range(T):
                ve.scalar_tensor_tensor(out=x[:, t], in0=x[:, t], scalar=stat[:, RSTD + t:RSTD + t + 1], in1=row[:],
                                        op0=ALU.mult, op1=ALU.mult).then_inc(x_ok, 1)
            residuals[0] += 1
            v_.wait_ge(x_ok, 2 * residuals[0])
            square_0(5)
            scale_0(5)
            operand(6, vecs[:, MIX_V:MIX_V + KD])
            with v_.Fori(0, 5) as turn:
                for j in range(LOOP):
                    low(IN_C + SPL + j, turn)
            for j in range(6):
                low(IN_C + 40 + SPL + j)
            if stop < 8:
                return

            rotate(1536, 24, rope_c_sb, rope_tc, 15)
            for f in range(6):
                if f % 2 == 0:
                    v_.wait_ge(c_qkt, f + 1)
                    ve.tensor_copy(qkT[:, 2 * f:2 * f + 2], bank[4 + f % 4][:].rearrange("p (k s) -> p k s", k=2)).then_inc(c_qkd, 1)
            v_.wait_ge(late_in[2], 32)
            v_.wait_ge(gm_mm, 1)
            for t in range(T):
                for gp in range(2):
                    last = ve.tensor_tensor(y_c[:, t, 384 * gp:384 * gp + 384], bank[2 * t + gp][:, 0:384],
                                            gmlp_row[:, 384 * gp:384 * gp + 384], ALU.mult)
            link(last)
            for t in range(T):
                for g in range(4):
                    y = y_c[:, t, 192 * g:192 * g + 192]
                    last = ve.scalar_tensor_tensor(out=y, in0=y, scalar=vecs[:, BSP_V + g:BSP_V + g + 1],
                                                   in1=proj[:, t, 192 * g:192 * g + 192], op0=ALU.add, op1=ALU.mult)
            last.then_inc(gm_y, 1)
            for i in range(5):
                if i < 4:
                    v_.wait_ge(c_sc, i + 1)
                    if i >= 2:
                        v_.wait_ge(c_pt, i - 1)
                    for t, (first, width) in enumerate(((0, P), (384, S))):
                        for g in range(3):
                            c0 = first + g * width
                            last = ve.scalar_tensor_tensor(out=prob_c[:, i % 2, c0:c0 + width], in0=bank[g][:, t * S:t * S + width],
                                                           scalar=0.125, in1=mask_sb[:, c0:c0 + width], op0=ALU.mult, op1=ALU.add)
                    link(last)
                    for t, (first, width) in enumerate(((0, 384), (384, 768))):
                        n = MX + 2 * i + t
                        last = ve.tensor_reduce(stat[:, n:n + 1], prob_c[:, i % 2, first:first + width], AX.X, ALU.max)
                    link(last)
                    ve.tensor_scalar(stat[:, NMX + 2 * i:NMX + 2 * i + 2], stat[:, MX + 2 * i:MX + 2 * i + 2], -1.0, None,
                                     ALU.mult).then_inc(c_sm, 1)
                if i >= 1:
                    h = i - 1
                    v_.wait_ge(c_pv, h + 1)
                    den = stat[:, DEN + 2 * h:DEN + 2 * h + 2]
                    link(ve.reciprocal(den, den))
                    for t in range(T):
                        last = ve.tensor_scalar(y_c[:, t, 768 + 64 * h:768 + 64 * h + 64], bank[6 + h % 2][:, t * 64:t * 64 + 64],
                                                den[:, t:t + 1], None, ALU.mult)
                        if h == 3:
                            last.then_inc((xn0, xn1)[t], 1)
                    if h < 3:
                        last.then_inc(c_o, 1)
            operand(7)
            for m in range(BR_A, BR_B):
                low(m + SPL)
            v_.wait_ge(sig_g, 1)
            v_.wait_ge(mm_done, BR_B)
            for t in range(T):
                for n in range(2):
                    ve.tensor_tensor(merged[:, t, n * CH:(n + 1) * CH], bank[2 * n + t][:],
                                     proj[:, t, 3840 + n * CH:3840 + (n + 1) * CH], ALU.mult)
            for m in range(BR_B, OUT_C):
                low(m + SPL)
            v_.wait_ge(mm_done, OUT_C)
            for t in range(T):
                for n in range(2):
                    last = ve.tensor_tensor(merged_b[:, 2 * t + n], bank[4 + 2 * n + t][:],
                                            proj[:, t, 4864 + n * CH:4864 + (n + 1) * CH], ALU.mult)
            link(last)
            for t in range(T):
                m2 = merged[:, t]
                ve.tensor_tensor(m2, m2, merged_b[:, 2 * t:2 * t + 2].rearrange("p n c -> p (n c)"), ALU.add).then_inc(
                    (xn0, xn1)[t], 1)
            operand(8)
            for m in range(OUT_C, UP_C):
                low(m + SPL)
            residual(UP_C, None)
            if stop < 9:
                return
            square_0(6)
            scale_0(6)
            operand(9, vecs[:, FFN_V:FFN_V + KD])

            def conv(c, b, turn=None):
                v_.wait_ge(av_t, at(c + 1, turn, 2))
                a = bank[4 + b][:].rearrange("p (k s) -> p k s", k=2)
                for tap in (2, 1, 0):
                    d = 2 - tap
                    for k in range(2):
                        w = vecs[:, cols(CONV_V + KF * tap + 2 * c + k, turn, 4, 1)]
                        o = conv_t[:, b, k]
                        if tap == 2:
                            last = ve.tensor_scalar(o, a[:, k], w, vecs[:, cols(CONV_V + KF * 3 + 2 * c + k, turn, 4, 1)],
                                                    ALU.mult, ALU.add)
                        else:
                            last = ve.scalar_tensor_tensor(out=o[:, d:S], in0=a[:, k, 0:S - d], scalar=w, in1=o[:, d:S],
                                                           op0=ALU.mult, op1=ALU.add)
                    if tap:
                        last.then_inc(dve_conv, 1)
                        v_.wait_ge(dve_conv, at(2 * c + d + 1, turn, 4))
                last.then_inc(conv_ok, 1)

            def conv_glu(c, b, turn=None):
                v_.wait_ge(gelu_ok, at(c + 1, turn, 2))
                ve.tensor_tensor(conv_t[:, b], bank[6 + b][:].rearrange("p (k s) -> p k s", k=2), conv_t[:, b],
                                 ALU.mult).then_inc(cu_ok, 1)

            def c_low(c, b, turn=None):
                v_.wait_ge(c_hi, at(c + 1, turn, 2))
                ve.tensor_tensor(u_lo[:, cols(2 * c, turn, 4, 2), :], conv_t[:, b],
                                 u_hi[:, cols(2 * c, turn, 4, 2), :].bitcast(F32), ALU.subtract).then_inc(c_lo, 1)

            for j in range(4):
                low(UP_C + SPL + j)
            with v_.Fori(0, 5) as turn:
                for j in range(LOOP):
                    low(UP_C + 4 + SPL + j, turn)
                    if j % 4 == 1:
                        conv(j // 4, j // 4, turn)
                    if j % 4 == 2:
                        conv_glu(j // 4, j // 4, turn)
                    if j % 4 == 3:
                        c_low(j // 4, j // 4, turn)
            for k in range(KF):
                low(DOWN_C + SPL + k)
                if k == 1:
                    conv(NCH_FF - 1, 0)
                if k == 2:
                    conv_glu(NCH_FF - 1, 0)
                if k == 3:
                    c_low(NCH_FF - 1, 0)
            residual(END, None)
            square_0(7)
            v_.wait_ge(late_in[3], 16)
            v_.wait_ge(rstd_ok, 8)
            for t in range(T):
                ve.scalar_tensor_tensor(out=x[:, t], in0=x[:, t], scalar=stat[:, RSTD + t:RSTD + t + 1], in1=row[:],
                                        op0=ALU.mult, op1=ALU.mult).then_inc(out_ok, 1)

        @block.tensor
        def _(pe):
            mm = nc.tensor.matmul

            def wide(m, u, b, v, turn=None, wait_operand=False):
                if wait_operand:
                    pe.wait_ge(h_lo_ok, 4 * v + u + 1)
                pe.wait_ge(lo_done, at(m + 1, turn, LOOP))
                s = m % SPL
                for t in range(T):
                    o = bank[2 * b + t][:]
                    for k in range(2):
                        hi, lo = (h[:, 2 * u + k, t * P:(t + 1) * P] for h in (h_hi, h_lo))
                        mm(o, hi, w_hi[:, s, k], start=(u == 0 and k == 0), stop=False)
                        mm(o, hi, w_lo[:, s, k], start=False, stop=False)
                        last = mm(o, lo, w_hi[:, s, k], start=False, stop=(u == 3 and k == 1))
                last.then_inc(mm_done, 1)

            def tall(m, a_hi, a_lo, k, first, last_k, base=0, order=(0, 1), wait_zero=None):
                pe.wait_ge(lo_done, m + 1)
                s = m % SPL
                for n in order:
                    if n == 0 and wait_zero is not None:
                        pe.wait_ge(*wait_zero)
                    for t in range(T):
                        o = bank[base + 2 * n + t][:]
                        hi, lo = (h[:, k, t * P:(t + 1) * P] for h in (a_hi, a_lo))
                        mm(o, hi, w_hi[:, s, n], start=first, stop=False)
                        mm(o, hi, w_lo[:, s, n], start=False, stop=False)
                        last = mm(o, lo, w_hi[:, s, n], start=False, stop=last_k)
                last.then_inc(mm_done, 1)

            def transposes(v, src):
                pe.wait_ge(xn0, v + 1)
                for kk in range(4):
                    for t in range(T):
                        if kk == 0 and t == 1:
                            pe.wait_ge(xn1, v + 1)
                        for k in range(2):
                            last = nc.tensor.transpose(bank[4 + kk][:, k * S + t * P:k * S + (t + 1) * P],
                                                       src[:, t, (2 * kk + k) * P:(2 * kk + k + 1) * P], ident[:])
                    last.then_inc(t_done, 1)

            def reduce_group(g, turn=None):
                pe.wait_ge(ada_done, at(8 * (g + 1), turn, 16))
                if g:
                    pe.wait_ge(ada_col, at(g, turn, 2))
                for q in range(4):
                    last = mm(bank[6][:, q:q + 1], ada_acc[:, g % 2, q * P:(q + 1) * P], ones[:, 0:1], start=True, stop=True)
                last.then_inc(ada_red, 1)

            def reduce_step(base, j, turn=None):
                if j == 4:
                    reduce_group(base // 4, turn)
                if j == 7:
                    reduce_group(base // 4 + 1, turn)

            def gate(n, h):
                pe.wait_ge(gate_diag, 2 * n + h + 1)
                if 2 * n + h:
                    pe.wait_ge(gate_ok, 2 * n + h)
                mm(bank[7][:], ones[:], diag[:].rearrange("p k s -> p (k s)"), start=True, stop=True).then_inc(gate_mm, 1)

            pe.wait_ge(const_ok, 4)
            pe.wait_ge(c_load, 16)
            nc.tensor.transpose(bank[5][:, 0:KD], c_rows[:], ident[0:KD, 0:KD]).then_inc(setup_t, 1)
            pe.wait_ge(vec_in, 16 * VECS)
            nc.tensor.transpose(bank[7][:, 0:53], stage_v[0:53, 0, :], ident[0:53, 0:53])
            nc.tensor.transpose(bank[7][:, CONV_V:CONV_V + 88], stage_v[0:88, 1, :], ident[0:88, 0:88])
            nc.tensor.transpose(bank[7][:, ADAB_V:ADAB_V + 96], stage_v[0:96, 2, :], ident[0:96, 0:96]).then_inc(setup_t, 1)
            reduce_group(0)
            reduce_group(1)
            reduce_group(2)
            reduce_group(3)
            pe.wait_ge(setup_p, 1)
            pe.wait_ge(ada_col, 4)
            for g in range(4):
                last = nc.tensor.transpose(bank[6][:, g * P:(g + 1) * P], w_sp[:, g], ident[:])
            last.then_inc(setup_t, 1)
            if stop < 1:
                return
            pe.wait_ge(setup, 4)
            transposes(0, xn)
            for j in range(LOOP):
                wide(QKV_A + j, j % 4, j // 4, 0, wait_operand=True)
                reduce_step(16, j)
            with pe.Fori(0, 2) as turn:
                for j in range(LOOP):
                    if j % 4 == 0:
                        pe.wait_ge(evac, at(1 + j // 4, turn, 2))
                    wide(QKV_A + 8 + j, j % 4, j // 4, 0, turn)
                    reduce_step(24, j, turn)
            gate(0, 0)
            gate(0, 1)
            if stop < 2:
                return

            pe.wait_ge(rope_ok, 1)
            pe.wait_ge(gate_ok, 2)
            for n, f in enumerate((0, 4, 1, 5, 2, 6, 3, 7)):
                if n >= 4:
                    pe.wait_ge((qk_d, qk_a)[n % 2], n // 2 - 1)
                for k in range(2):
                    for t in range(T):
                        last = nc.tensor.transpose(bank[4 + n % 4][:, k * S + t * P:k * S + (t + 1) * P],
                                                   proj[:, t, (2 * f + k) * P:(2 * f + k + 1) * P], ident[:])
                last.then_inc(qk_t, 1)
            NH = 8
            for i in range(NH + 2):
                if i < NH:
                    if i % 2 == 0:
                        pe.wait_ge(qk_d, i // 2 + 1)
                        pe.wait_ge(qk_a, i // 2 + 1)
                    if i == 0:
                        pe.wait_ge(evac, 6)
                    if i >= 2:
                        pe.wait_ge(exp_ok, i - 1)
                    for c in range(2):
                        for t in range(T):
                            last = mm(bank[2 * (i % 2) + c][:, t * S:(t + 1) * S], qkT[64 * c:64 * c + 64, i, t * P:(t + 1) * P],
                                      qkT[64 * c:64 * c + 64, 8 + i, :], start=True, stop=True)
                    last.then_inc(sc_ok, 1)
                if 1 <= i <= NH:
                    h = i - 1
                    pe.wait_ge(wgt_ok, h + 1)
                    if h == 0:
                        pe.wait_ge(qk_d, 4)
                        pe.wait_ge(qk_a, 4)
                    if h >= 2:
                        pe.wait_ge(wgt_ev, h - 1)
                    for t in range(T):
                        for k in range(2):
                            last = nc.tensor.transpose(bank[4 + h % 2][:, k * S + t * P:k * S + (t + 1) * P],
                                                       wgt[:, h % 2, t, k * P:(k + 1) * P], ident[:])
                    last.then_inc(wgt_t, 1)
                if i >= 2:
                    h = i - 2
                    pe.wait_ge(wgt_ev, h + 1)
                    if h >= 2:
                        pe.wait_ge(o_ok, h - 1)
                    for t in range(T):
                        for k in range(2):
                            last = mm(bank[6 + h % 2][:, t * P:(t + 1) * P], wgtT[:, h % 2, k, t * P:(t + 1) * P],
                                      proj[:, k, 2048 + h * P:2048 + (h + 1) * P], start=(k == 0), stop=(k == 1))
                    last.then_inc(pv_ok, 1)
            transposes(1, att)
            for k in range(KD):
                pe.wait_ge(h_lo_ok, 4 * 1 + k // 2 + 1)
                tall(WO_A + k, h_hi, h_lo, k, k == 0, k == KD - 1)
            if stop < 3:
                return
            transposes(2, xn)

            def u_transpose(f, c, b, turn=None):
                pe.wait_ge(u_ok, at(NCH_FF * f + c + 1, turn, 2))
                for k in range(2):
                    for t in range(T):
                        last = nc.tensor.transpose(bank[4 + b][:, k * S + t * P:k * S + (t + 1) * P],
                                                   act_u[:, b, t, k * P:(k + 1) * P], ident[:])
                last.then_inc(u_t, 1)

            def feed_forward(base, f, v, gate_n, with_ada):
                for u in range(4):
                    wide(base + u, u, 0, v, wait_operand=True)
                with pe.Fori(0, 5) as turn:
                    for j in range(LOOP):
                        if j % 4 == 3:
                            u_transpose(f, j // 4, j // 4, turn)
                        wide(base + 4 + j, j % 4, 1 - j // 4, v, turn)
                        if with_ada:
                            reduce_step(40, j, turn)
                down = base + 4 * NCH_FF
                for k in range(KF):
                    if k == 3:
                        u_transpose(f, NCH_FF - 1, 0)
                    if k % 2 == 0:
                        pe.wait_ge(u_lo_ok, NCH_FF * f + k // 2 + 1)
                    tall(down + k, u_hi, u_lo, k, k == 0, k == KF - 1, order=(1, 0),
                         wait_zero=(u_ok, NCH_FF * (f + 1)) if k == 0 else None)
                    if with_ada and k < 16:
                        reduce_step(80 + k // 8 * 8, k % 8)
                    if k == 4:
                        gate(gate_n, 0)
                    if k == 6:
                        gate(gate_n, 1)

            feed_forward(IN_0, 0, 2, 1, True)
            if stop < 4:
                return
            transposes(3, xn)
            for j in range(12):
                if j == 8:
                    pe.wait_ge(evac, 7)
                wide(QKV_B + j, j % 4, j // 4 % 2, 3, wait_operand=j < 4)
            gate(2, 0)
            gate(2, 1)
            if stop < 5:
                return

            pe.wait_ge(rope_ok, 2)
            pe.wait_ge(gate_ok, 6)
            for f in range(5):
                if f >= 4:
                    pe.wait_ge(qk_d, 4 + f // 2 - 1)
                for k in range(2):
                    for t in range(T):
                        last = nc.tensor.transpose(bank[4 + f % 4][:, k * S + t * P:k * S + (t + 1) * P],
                                                   proj[:, t, (2 * f + k) * P:(2 * f + k + 1) * P], ident[:])
                last.then_inc(qk_t, 1)
            pe.wait_ge(qk_d, 7)
            pe.wait_ge(qk_a, 6)
            for i in range(NH + 1):
                if i < NH:
                    if i >= 4:
                        pe.wait_ge(exp_ok, 8 + i - 3)
                    for t in range(T):
                        last = mm(bank[i % 4][:, t * S:(t + 1) * S], qkT[:, i, t * P:(t + 1) * P], qkT[:, 8 + i // 4, :],
                                  start=True, stop=True)
                    last.then_inc(sc_ok, 1)
                if i >= 1:
                    h = i - 1
                    pe.wait_ge(exp_ok, 8 + h + 1)
                    if h >= 2:
                        pe.wait_ge(wgt_ev, 8 + h - 1)
                    for t in range(T):
                        for k in range(2):
                            last = nc.tensor.transpose(bank[4 + h % 2][:, k * S + t * P:k * S + (t + 1) * P],
                                                       prob_b[:, h % 2, t, k * P:(k + 1) * P], ident[:])
                    last.then_inc(wgt_t, 1)
                    pe.wait_ge(wgt_ev, 8 + h + 1)
                    if h >= 2:
                        pe.wait_ge(o_ok, 8 + h - 1)
                    v0 = 1280 + h // 4 * P
                    for t in range(T):
                        for k in range(2):
                            last = mm(bank[6 + h % 2][:, t * P:(t + 1) * P], probT_b[:, h % 2, k, t * P:(t + 1) * P],
                                      proj[:, k, v0:v0 + P], start=(k == 0), stop=(k == 1))
                    last.then_inc(pv_ok, 1)
            transposes(4, att_b)
            for k in range(KD):
                pe.wait_ge(h_lo_ok, 4 * 4 + k // 2 + 1)
                tall(WO_B + k, h_hi, h_lo, k, k == 0, k == KD - 1)
            if stop < 6:
                return
            transposes(5, xn)
            feed_forward(IN_1, 1, 5, 3, False)
            if stop < 7:
                return

            transposes(6, xn)
            for kk in range(1, 5):
                pe.wait_ge(h_lo_ok, 4 * 6 + kk)
            with pe.Fori(0, 5) as turn:
                for j in range(LOOP):
                    if j % 4 == 0:
                        pe.wait_ge(evac, at(9 + j // 4 - 1, turn, 2))
                    wide(IN_C + j, j % 4, j // 4, 6, turn)
            pe.wait_ge(evac, 9 + 9)
            for u in range(4):
                wide(IN_C + 40 + u, u, 0, 6)
            pe.wait_ge(evac, 9 + 10)
            for j in range(2):
                m = TAIL_C + j
                pe.wait_ge(lo_done, m + 1)
                whi, wlo = (w[:, m % SPL].rearrange("p a (b n) -> p (a b) n", b=2) for w in (w_hi, w_lo))
                for t in range(T):
                    o = bank[2 + t][:, 0:HC]
                    for k in range(4):
                        hi, lo = (h[:, 4 * j + k, t * P:(t + 1) * P] for h in (h_hi, h_lo))
                        mm(o, hi, whi[:, k], start=(j == 0 and k == 0), stop=False)
                        mm(o, hi, wlo[:, k], start=False, stop=False)
                        last = mm(o, lo, whi[:, k], start=False, stop=(j == 1 and k == 3))
                last.then_inc(mm_done, 1)
            if stop < 8:
                return
            pe.wait_ge(rope_ok, 3)
            for f in range(6):
                if f >= 4:
                    pe.wait_ge((c_qkd, c_qka)[f % 2], f // 2 - 1)
                for k in range(2):
                    for t in range(T):
                        last = nc.tensor.transpose(bank[4 + f % 4][:, k * S + t * P:k * S + (t + 1) * P],
                                                   proj[:, t, 1536 + (2 * f + k) * P:1536 + (2 * f + k + 1) * P], ident[:])
                last.then_inc(c_qkt, 1)
            pe.wait_ge(gm_v, 1)
            pe.wait_ge(evac, 9 + 12)
            for t in range(T):
                for g in range(4):
                    last = mm(bank[2 * t + g // 2][:, g % 2 * 192:g % 2 * 192 + 192], w_spT[:, g],
                              proj[:, t, 768 + 192 * g:768 + 192 * g + 192], start=True, stop=True)
            last.then_inc(gm_mm, 1)
            pe.wait_ge(c_qkd, 3)
            pe.wait_ge(c_qka, 3)
            pe.wait_ge(gm_y, 1)
            for i in range(5):
                if i < 4:
                    if i >= 1:
                        pe.wait_ge(c_sm, i)
                    r0 = i % 2 * 64
                    for g in range(3):
                        q = (4 * g + i) // 2
                        for t, width in enumerate((P, S)):
                            last = mm(bank[g][:, t * S:t * S + width], qkT[r0:r0 + 64, q, t * P:(t + 1) * P],
                                      qkT[r0:r0 + 64, 6 + q, 0:width], start=True, stop=True)
                    last.then_inc(c_sc, 1)
                if i >= 1:
                    h = i - 1
                    pe.wait_ge(c_exp, h + 1)
                    if h >= 1:
                        pe.wait_ge(c_pev, h)
                    tiles = [(0, g, 0, g * P) for g in range(3)]
                    tiles += [(1, g, k, 384 + g * S + k * P) for g in range(3) for k in range(2)]
                    for n, (t, g, k, c0) in enumerate(tiles):
                        last = nc.tensor.transpose(bank[3 + n // 4][:, n % 4 * P:(n % 4 + 1) * P], prob_c[:, h % 2, c0:c0 + P],
                                                   ident[:])
                    last.then_inc(c_pt, 1)
                    pe.wait_ge(c_pev, h + 1)
                    if h >= 2:
                        pe.wait_ge(c_o, h - 1)
                    for n, (t, g, k, c0) in enumerate(tiles):
                        v0 = 3072 + 64 * (4 * g + h)
                        last = mm(bank[6 + h % 2][:, t * 64:t * 64 + 64], probT_c[:, n], proj[:, k, v0:v0 + 64],
                                  start=(n in (0, 3)), stop=(n in (2, 8)))
                    last.then_inc(c_pv, 1)
            transposes(7, y_c)
            for k in range(6):
                pe.wait_ge(h_lo_ok, 4 * 7 + k // 2 + 1)
                tall(BR_A + k, h_hi, h_lo, k, k == 0, k == 5)
            pe.wait_ge(h_lo_ok, 4 * 7 + 4)
            for k in range(2):
                tall(BR_B + k, h_hi, h_lo, 6 + k, k == 0, k == 1, base=4)
            transposes(8, merged)
            for k in range(KD):
                pe.wait_ge(h_lo_ok, 4 * 8 + k // 2 + 1)
                tall(OUT_C + k, h_hi, h_lo, k, k == 0, k == KD - 1)
            if stop < 9:
                return
            transposes(9, xn)

            def av_transpose(c, b, turn=None):
                pe.wait_ge(av_ok, at(c + 1, turn, 2))
                for half_, bk in enumerate((4 + b, 6 + b)):
                    for k in range(2):
                        for t in range(T):
                            c0 = half_ * HC + k * P
                            last = nc.tensor.transpose(bank[bk][:, k * S + t * P:k * S + (t + 1) * P], av[:, b, t, c0:c0 + P],
                                                       ident[:])
                last.then_inc(av_t, 1)

            for u in range(4):
                wide(UP_C + u, u, 0, 9, wait_operand=True)
            with pe.Fori(0, 5) as turn:
                for j in range(LOOP):
                    if j % 4 == 1:
                        av_transpose(j // 4, j // 4, turn)
                    wide(UP_C + 4 + j, j % 4, 1 - j // 4, 9, turn)
            for k in range(KF):
                if k == 1:
                    av_transpose(NCH_FF - 1, 0)
                if k % 2 == 0:
                    pe.wait_ge(c_lo, k // 2 + 1)
                tall(DOWN_C + k, u_hi, u_lo, k, k == 0, k == KF - 1, order=(1, 0),
                     wait_zero=(av_ok, NCH_FF) if k == 0 else None)


_INPUTS = ["x", "c", "ada_w", "ada_b", "norm1_g", "norm2_g", "a_w_qkv", "a_w_o", "a_lam_q1", "a_lam_k1", "a_lam_q2",
           "a_lam_k2", "a_subln_g", "b_w_qkv", "b_w_o", "b_qnorm_g", "b_knorm_g", "f_w_in", "f_w_out", "final_g",
           "positions_2", "mix_norm_g_2", "w_in_2", "gmlp_norm_g_2", "w_spatial_2", "b_spatial_2", "w_branch_a_2",
           "w_branch_b_2", "w_out_2", "ffn_norm_g_2", "w_up_2", "conv_w_2", "conv_b_2", "w_down_2", "final_norm_g_2"]


def constants():
    f = np.float32

    def angles(pos, half, theta):
        freqs = (f(theta) ** (-np.arange(half, dtype=f) / f(half))).astype(f)
        a = (pos.astype(f)[:, None] * freqs[None, :]).astype(f)
        return np.cos(a).astype(f), np.sin(a).astype(f)

    tok = np.arange(S)
    cos, sin = angles(tok, 8, 500000.0)
    rope_a = np.stack([np.concatenate([cos, cos], 1), np.concatenate([-sin, sin], 1)], 1)
    cr, sr = angles(tok // 64, 32, 10000.0)
    cc, sc = angles(tok % 64, 32, 10000.0)
    rope_b = np.stack([np.concatenate([cr, cr, cc, cc], 1), np.concatenate([-sr, sr, -sc, sc], 1)], 1)
    inv_freq = (f(500000.0) ** (-np.arange(0, 16, 2, dtype=f) / f(16))).astype(f)
    i, j = tok[:, None], tok[None, :]
    seen = [(i >= j) & (i - j <= 128 * d) & ((i - j) % d == 0) for d in (1, 4, 16)]
    far = [np.where(m, 0.0, -3e37).astype(f) for m in seen]
    masks = np.concatenate([m[:P, :P] for m in far] + [m[P:, :] for m in far], 1)
    return {"rope_a": rope_a.astype(f), "rope_b": rope_b.astype(f), "inv_freq": inv_freq, "masks": masks}


def kernel(**inputs):
    import concourse.bacc as bacc
    from concourse.bass_utils import run_bass_kernel_spmd

    nc = bacc.Bacc("TRN2", target_bir_lowering=False, num_devices=1)
    arrays, args = {}, []
    for name, a in [(n, np.ascontiguousarray(inputs[n])) for n in _INPUTS] + list(constants().items()):
        arrays["in_" + name] = a
        args.append(nc.dram_tensor("in_" + name, a.shape, mybir.dt.from_np(a.dtype), kind="ExternalInput").ap())
    out = nc.dram_tensor("out", (1, S, D), F32, kind="ExternalOutput").ap()
    program(nc, *args, out)
    r = run_bass_kernel_spmd(nc, [arrays], core_ids=[0])
    return r.results[0]["out"]
```

```python
import math
from contextlib import ExitStack

import numpy as np

import concourse.bass as bass
from concourse import mybir

F32 = mybir.dt.float32
F32R = mybir.dt.float32r
I32 = mybir.dt.int32
ALU = mybir.AluOpType
ACT = mybir.ActivationFunctionType
AX = mybir.AxisListType

P = 128
D = 1024
S = 256
T = S // P
KD = D // P
FF = 2816
KF = FF // P
CH = 512
HC = CH // 2
NCH_FF = FF // HC
EPS = 1e-6
SIDE = 8
VECS = 11
W2_COLS = 5888
LAM_INIT = 0.8 - 0.6 * math.exp(-0.3 * 0)
TWO_PI = 2 * math.pi
ROUND = 1.5 * 2.0 ** 23

QKV_A, WO_A, IN_0, OUT_0, QKV_B, WO_B, IN_1, OUT_1 = 0, 24, 32, 76, 98, 110, 118, 162
IN_C, TAIL_C, BR_A, BR_B, OUT_C, UP_C, DOWN_C, END = 184, 228, 230, 236, 238, 246, 290, 312
RAW = 8
SPL = 4
LOOP = 8

ADA_SLOTS = 4
GROUPS = 24
LOOP_FOLD, LOOP_REDUCE, LOOP_TAKE = {0: 0, 2: 1, 3: 2, 5: 3}, {7: 0}, {7: 0}
OUT_FOLD = {5 * (n // 4) + n % 4: n for n in range(16)}
OUT_REDUCE, OUT_TAKE = {5 + 5 * g: g for g in range(4)}, {6 + 5 * g: g for g in range(4)}

QK_STEPS_A = (19, 20, 21, 22)
QK_ORDER_A = (0, 4, 1, 5, 2, 6, 3, 7)
HEADS_A = ((0, 4), (4, 7), (7, 8))
CHUNKS_B = (2, 0, 1)
K_STEP_B, K_SCALE_STEP_B, K_TURN_STEP_B, Q_STEP_B = 4, 6, 8, 8
B_REDUCE, B_TAKE = {9: 0}, {10: 0}
SPATIAL_STEP, QK_STEPS = 26, (28, 29, 30)
SCORE_STEPS, PROBT_STEPS, PV_STEPS = (33, 36, 39, 42), (35, 38, 41, 44), (37, 40, 43, 46)


def c_bank(c):
    return c % 2 if c < 8 else 0


def first_steps(steps, n):
    return {step: index for step, index in steps.items() if index < n}


def at(const, turn=None, per=0):
    return const if turn is None else const + turn * per


def cols(start, turn, per, size):
    return slice(start, start + size) if turn is None else bass.ds(turn * per + start, size)


def program(nc, x_in, c_in, ada_w, ada_b, norm1_g, norm2_g, a_w_qkv, a_w_o, lq1, lk1, lq2, lk2,
            subln_g, b_w_qkv, b_w_o, qnorm_g, knorm_g, f_w_in, f_w_out, final_g, positions,
            mix_g, w_in_c, gmlp_g, w_spatial, b_spatial, w_branch_a, w_branch_b, w_out_c, ffn_g_c,
            w_up_c, conv_w, conv_b, w_down_c, final_g_c, rope_a, rope_b, inv_freq, masks, out):
    ctx = ExitStack()
    with ctx:
        def sem(name):
            return ctx.enter_context(nc.semaphore(name))

        def sb(name, shape, dt=F32):
            return ctx.enter_context(nc.sbuf_tensor(name, shape, dt))

        raw = sb("raw", [P, RAW, 2, CH])
        ada = sb("ada", [P, ADA_SLOTS, 2, CH])
        w_hi = sb("w_hi", [P, SPL, 2, CH], F32R)
        w_lo = sb("w_lo", [P, SPL, 2, CH], F32R)
        h_hi = sb("h_hi", [P, KD, S], F32R)
        h_lo = sb("h_lo", [P, KD, S], F32R)
        x = sb("x", [P, T, D])
        ident = sb("ident", [P, P])
        ones = sb("ones", [P, P])
        vecs = sb("vecs", [P, 237])
        cond = sb("cond", [P, KD])
        half = sb("half", [P, 20])
        mod = sb("mod", [P, 4 * GROUPS])
        gains = sb("gains", [P, KD])
        stat = sb("stat", [P, 176])
        ada_acc = sb("ada_acc", [P, 2, CH])
        gate_row = sb("gate_row", [P, D])
        rope_a_sb = sb("rope_a_sb", [P, T, 2, 16])
        rope_c_sb = sb("rope_c_sb", [P, T, 2, 16])
        w_spT = sb("w_spT", [P, 4, P])
        REG_U = 2 * KF * S * 4
        REG_P = T * W2_COLS * 4
        u_base = nc.sbuf_base
        u_base = (u_base + 63) // 64 * 64
        p_base = u_base + REG_U
        arena = sb("arena", [P, (REG_U + REG_P) // 4 + 16])

        def at_u(name, shape, first, dt=F32):
            return nc.alloc_sbuf_tensor_at(name, shape, dt, offset=u_base + 4 * first)

        def at_p(name, shape, first, dt=F32):
            return nc.alloc_sbuf_tensor_at(name, shape, dt, offset=p_base + 4 * first)

        u_hi = at_u("u_hi", [P, KF, S], 0, F32R)
        u_lo = at_u("u_lo", [P, KF, S], KF * S, F32R)
        qkT = at_u("qkT", [P, 16, S], 0)
        prob_a = at_u("prob_a", [P, 2, 2, T, S], 4096)
        rope_t = at_u("rope_t", [P, T, 32, 16], 4096)
        wgt = at_u("wgt", [P, 2, T, S], 6144)
        wgtT = at_u("wgtT", [P, 2, T, S], 7168)
        att = at_u("att", [P, T, D], 8192)
        ada_prod = at_u("ada_prod", [P, 2, CH], 10240)
        swap_b = at_u("swap_b", [P, T, 10, P], 2560)
        prob_b = at_u("prob_b", [P, 2, T, S], 5120)
        probT_b = at_u("probT_b", [P, 2, T, S], 6144)
        rope_b_sb = at_u("rope_b_sb", [P, T, 2, P], 7168)
        gain_b = at_u("gain_b", [P, 2, P], 7680)
        table_b = at_u("table_b", [P, T, 2, 2, P], 7936)
        mask_sb = at_u("mask_sb", [P, 1152], 3072)
        prob_c = at_u("prob_c", [P, 2, 1152], 4224)
        probT_c = at_u("probT_c", [P, 9, P], 6528)
        y_c = at_u("y_c", [P, T, D], 7680)
        gmlp_row = at_u("gmlp_row", [P, 768], 9728)
        rope_tc = at_u("rope_tc", [P, T, 24, 16], 10496)
        proj = at_p("proj", [P, T, W2_COLS], 0)
        xn = at_p("xn", [P, T, D], 0)
        att_b = at_p("att_b", [P, T, D], 2048)
        hf = at_p("hf", [P, KD, S], 2048)
        res = at_p("res", [P, 2 * T, CH], 4096)
        act_s = at_p("act_s", [P, 2, T, HC], 6144)
        act_u = at_p("act_u", [P, 2, T, HC], 7168)
        av = at_p("av", [P, 2, T, CH], 6144)
        conv_t = at_p("conv_t", [P, 2, 2, S], 8192)
        row = at_p("row", [P, D], 9216)
        diag = at_p("diag", [P, 4, P], 10240)
        stage_v = at_p("stage_v", [P, 3, P], 10752)
        lam_v = at_p("lam_v", [P, 4, 64], 11136)
        w_sp = at_p("w_sp", [P, 4, P], 9216)
        freq_row = at_p("freq_row", [P, 8], 11392)
        pos_i = at_p("pos_i", [P, T], 11400, I32)
        pos_f = at_p("pos_f", [P, T], 11408)
        ang = at_p("ang", [P, T, 8], 11416)
        ang_n = at_p("ang_n", [P, T, 2, 8], 11432)
        ang_r = at_p("ang_r", [P, T, 2, 8], 11464)
        c_rows = at_p("c_rows", [KD, P], 11504)
        merged = at_p("merged", [P, T, D], 0)
        merged_b = at_p("merged_b", [P, 2 * T, CH], W2_COLS)

        bank = [ctx.enter_context(nc.psum_tensor(f"bank{n}", [P, CH], F32)) for n in range(8)]

        N1_V, N2_V, MIX_V, FFN_V, SUB_V, BSP_V, CONV_V, ADAB_V = 0, 16, 32, 40, 48, 49, 53, 141
        SS, RSTD, MX, NMX, DEN, RDEN, MISC = 0, 20, 40, 72, 104, 136, 168
        neg_lam = stat[:, MISC:MISC + 1]

        raw_in = [sem(f"raw_in{n}") for n in range(RAW)]
        ada_in = [sem(f"ada_in{n}") for n in range(ADA_SLOTS)]
        hi_done = sem("hi_done")
        lo_done = sem("lo_done")
        mm_done = sem("mm_done")
        ada_done = sem("ada_done")
        prod_ok = sem("prod_ok")
        ada_red = sem("ada_red")
        ada_col = sem("ada_col")
        c_load = sem("c_load")
        vec_in = sem("vec_in")
        side_in = sem("side_in")
        x_load = sem("x_load")
        late_in = [sem(f"late_in{n}") for n in range(4)]
        const_ok = sem("const_ok")
        setup = sem("setup")
        setup_v = sem("setup_v")
        setup_t = sem("setup_t")
        setup_p = sem("setup_p")
        dve = sem("dve")
        dve_conv = sem("dve_conv")
        sq0, sq1 = sem("sq0"), sem("sq1")
        rstd_ok = sem("rstd_ok")
        xn0, xn1 = sem("xn0"), sem("xn1")
        pre_tmp = sem("pre_tmp")
        t_done = sem("t_done")
        hf_ok = sem("hf_ok")
        h_hi_ok, h_lo_ok = sem("h_hi_ok"), sem("h_lo_ok")
        res_ok = sem("res_ok")
        x_ok = sem("x_ok")
        evac = sem("evac")
        gate_diag, gate_mm, gate_ok = sem("gate_diag"), sem("gate_mm"), sem("gate_ok")
        s_act = sem("s_act")
        u_ok = sem("u_ok")
        u_t = sem("u_t")
        u_hi_ok, u_lo_ok = sem("u_hi_ok"), sem("u_lo_ok")
        av_ok, av_t, conv_ok, gelu_ok, cu_ok, c_hi, c_lo = (
            sem(n) for n in ("av_ok", "av_t", "conv_ok", "gelu_ok", "cu_ok", "c_hi", "c_lo"))
        rope_ok = sem("rope_ok")
        qk_t = sem("qk_t")
        qk_d, qk_a = sem("qk_d"), sem("qk_a")
        sc_ok, nmx_ok, exp_ok, wgt_ok, wgt_t, wgt_ev, pv_ok, o_sq, o_ok = (
            sem(n) for n in ("sc_ok", "nmx_ok", "exp_ok", "wgt_ok", "wgt_t", "wgt_ev", "pv_ok", "o_sq", "o_ok"))
        qk_sq0, qk_sq1 = sem("qk_sq0"), sem("qk_sq1")
        qk_r = sem("qk_r")
        gm_sq, gm_r, gm_v, gm_mm, gm_y = (sem(n) for n in ("gm_sq", "gm_r", "gm_v", "gm_mm", "gm_y"))
        c_qkt, c_qkd, c_qka, c_sc, c_sm, c_exp, c_pt, c_pev, c_pv, c_o = (
            sem(n) for n in ("c_qkt", "c_qkd", "c_qka", "c_sc", "c_sm", "c_exp", "c_pt", "c_pev", "c_pv", "c_o"))
        gelu_z, sig_g, br_ok = sem("gelu_z"), sem("sig_g"), sem("br_ok")
        out_ok = sem("out_ok")
        stored = sem("stored")

        block = ctx.enter_context(nc.Block())

        @block.sync
        def _(sp):
            def slot_free(m, turn=None):
                if m >= RAW:
                    sp.wait_ge(lo_done, at(m - RAW + 1, turn, LOOP))

            def load_wide(m, w, u, c0, turn=None, n=CH, per=2 * CH):
                slot_free(m, turn)
                src = w.rearrange("(k p) n -> p k n", p=P)[:, 2 * u:2 * u + 2, cols(c0, turn, per, n)]
                sp.dma_start(raw[:, m % RAW], src).then_inc(raw_in[m % RAW], 32)

            def load_pair(m, w, u, c0, turn=None):
                slot_free(m, turn)
                v = w.rearrange("(k p) n -> p k n", p=P)
                for half in range(2):
                    src = v[:, 2 * u:2 * u + 2, cols(half * FF + c0, turn, CH, HC)]
                    sp.dma_start(raw[:, m % RAW, :, half * HC:(half + 1) * HC], src).then_inc(raw_in[m % RAW], 16)

            def load_tall(m, w, k):
                slot_free(m)
                sp.dma_start(raw[:, m % RAW], w[k * P:(k + 1) * P, :].rearrange("p (a n) -> p a n", a=2)).then_inc(
                    raw_in[m % RAW], 32)

            def load_ada(a, turn=None):
                g, u = divmod(a, 4)
                layer, g = divmod(g, 12)
                if a >= ADA_SLOTS:
                    sp.wait_ge(ada_done, at(2 * (a - ADA_SLOTS + 1), turn, 8))
                src = ada_w[layer].rearrange("(k p) n -> p k n", p=P)[:, 2 * u:2 * u + 2, cols(g * CH, turn, CH, CH)]
                sp.dma_start(ada[:, a % ADA_SLOTS], src).then_inc(ada_in[a % ADA_SLOTS], 16)

            def load_ada_step(base, j, turn=None, steps=LOOP_FOLD):
                if j in steps:
                    load_ada(base + steps[j], turn)

            sp.dma_start(c_rows[:], c_in[0].rearrange("(k p) -> k p", p=P)).then_inc(c_load, 16)
            for a in range(ADA_SLOTS):
                load_ada(a)
            for t in range(T):
                sp.dma_start(x[:, t], x_in[0, t * P:(t + 1) * P, :]).then_inc(x_load, 16)
            for a in range(ADA_SLOTS, 16):
                load_ada(a)
            for m in range(8):
                load_wide(m, a_w_qkv[0], m % 4, m // 4 * CH)
            with sp.Fori(0, 2) as turn:
                for j in range(LOOP):
                    load_ada_step(16, j, turn)
                    load_wide(8 + j, a_w_qkv[0], j % 4, 2 * CH + j // 4 * CH, turn)
            for j in range(8):
                load_ada_step(24, j)
                load_tall(WO_A + j, a_w_o[0], j)
            for a in range(28, 32):
                load_ada(a)
            for m in range(4):
                load_pair(IN_0 + m, f_w_in[0], m, 0)
            for a in range(32, 40):
                load_ada(a)
            for m in range(8):
                load_pair(IN_0 + 4 + m, f_w_in[0], m % 4, (1 + m // 4) * HC)
            for part in range(2):
                with sp.Fori(0, 2) as turn:
                    for j in range(LOOP):
                        load_ada_step(40 + 8 * part, j, turn)
                        load_pair(IN_0 + 12 + 16 * part + j, f_w_in[0], j % 4, (3 + 4 * part + j // 4) * HC, turn)
            for j in range(8):
                load_ada_step(56, j)
                load_tall(OUT_0 + j, f_w_out[0], j)
            for k in range(KF):
                load_ada_step(60, k, steps=OUT_FOLD)
                if k + 8 < KF:
                    load_tall(OUT_0 + 8 + k, f_w_out[0], 8 + k)
                else:
                    m = k + 8 - KF
                    load_wide(QKV_B + m, b_w_qkv[0], m % 4, CHUNKS_B[m // 4] * CH)
            for m in range(12):
                load_ada_step(76, m, steps=first_steps(OUT_FOLD, 8))
                if m < 4:
                    load_wide(QKV_B + 8 + m, b_w_qkv[0], m, CHUNKS_B[2] * CH)
                else:
                    load_tall(WO_B + m - 4, b_w_o[0], m - 4)
            for a in range(84, 88):
                load_ada(a)
            for m in range(4):
                load_pair(IN_1 + m, f_w_in[1], m, 0)
            with sp.Fori(0, 5) as turn:
                for j in range(LOOP):
                    load_pair(IN_1 + 4 + j, f_w_in[1], j % 4, (1 + j // 4) * HC, turn)
            for k in range(KF):
                if k >= 8:
                    load_ada_step(88, k - 8, steps=first_steps(OUT_FOLD, 8))
                load_tall(OUT_1 + k, f_w_out[1], k)
            with sp.Fori(0, 5) as turn:
                for j in range(LOOP):
                    load_wide(IN_C + j, w_in_c[0], j % 4, j // 4 * CH, turn)
            for j in range(4):
                load_wide(IN_C + 40 + j, w_in_c[0], j, 10 * CH)
            for j in range(2):
                slot_free(TAIL_C + j)
                src = w_in_c[0].rearrange("(k p) n -> p k n", p=P)[:, 4 * j:4 * j + 4, 11 * CH:W2_COLS]
                sp.dma_start(raw[:, (TAIL_C + j) % RAW].rearrange("p a (b n) -> p (a b) n", b=2), src).then_inc(
                    raw_in[(TAIL_C + j) % RAW], 32)
            for k in range(6):
                load_tall(BR_A + k, w_branch_a[0], k)
            for k in range(2):
                load_tall(BR_B + k, w_branch_b[0], k)
            for k in range(KD):
                load_tall(OUT_C + k, w_out_c[0], k)
            for m in range(4):
                load_pair(UP_C + m, w_up_c[0], m, 0)
            with sp.Fori(0, 5) as turn:
                for j in range(LOOP):
                    load_pair(UP_C + 4 + j, w_up_c[0], j % 4, (1 + j // 4) * HC, turn)
            for k in range(KF):
                load_tall(DOWN_C + k, w_down_c[0], k)
            for t in range(T):
                sp.wait_ge(out_ok, t + 1)
                sp.dma_start(out[0, t * P:(t + 1) * P, :], x[:, t]).then_inc(stored, 16)
            sp.wait_ge(stored, 16 * T)

        LOOPED = (4, 5, 6, 10, 11, 12, 13, 14)

        def acc_slot(g):
            return 0 if g in LOOPED else g % 2

        def sum_bank(g):
            return 0 if g < 4 else 6

        def last_in_slot(g):
            return g - 1 if g in LOOPED else max(n for n in range(g) if acc_slot(n) == acc_slot(g))

        @block.gpsimd
        def _(pool):
            power = [0]
            nc.gpsimd.memset(ident[:], 0.0).then_inc(const_ok, 1)
            nc.gpsimd.memset(ones[:], 1.0).then_inc(const_ok, 1)
            nc.gpsimd.memset(half[:], -0.5).then_inc(const_ok, 1)
            pool.wait_ge(const_ok, 3)
            nc.gpsimd.affine_select(out=ident[:], in_=ident[:], compare_op=ALU.not_equal, fill=1.0, base=0,
                                    pattern=[[-1, P]], channel_multiplier=1).then_inc(const_ok, 1)
            pool.dma_start(w_sp[:], w_spatial[0].rearrange("g t s -> t g s")).then_inc(side_in, 16)
            pool.wait_ge(side_in, 16)
            nc.gpsimd.affine_select(out=w_sp[:], in_=w_sp[:], compare_op=ALU.is_ge, fill=0.0, base=0,
                                    pattern=[[0, 4], [-1, P]], channel_multiplier=1).then_inc(setup_p, 1)
            def inv_sqrt(first, n, width):
                nc.gpsimd.tensor_scalar(stat[:, RSTD + first:RSTD + first + n], stat[:, SS + first:SS + first + n],
                                        1.0 / width, EPS, ALU.mult, ALU.add).then_inc(pre_tmp, 1)
                power[0] += 1
                pool.wait_ge(pre_tmp, power[0])
                return nc.gpsimd.tensor_tensor(stat[:, RSTD + first:RSTD + first + n],
                                               stat[:, RSTD + first:RSTD + first + n],
                                               half[:, 0:n], ALU.pow)

            def norm(v):
                for t in range(T):
                    pool.wait_ge((sq0, sq1)[t], v + 1)
                    inv_sqrt(t, 1, D).then_inc(rstd_ok, 1)

            added = [0]

            def fold(a):
                g = a // 4
                acc = ada_acc[:, acc_slot(g)]
                pool.wait_ge(ada_in[a % ADA_SLOTS], 16 * (a // ADA_SLOTS + 1))
                if a % 4 == 0:
                    pool.wait_ge(ada_red, last_in_slot(g) + 1)
                pool.wait_ge(ada_done, 2 * a)
                nc.gpsimd.tensor_tensor(ada_prod[:], ada[:, a % ADA_SLOTS],
                                        cond[:, 2 * (a % 4):2 * (a % 4) + 2].unsqueeze(2).to_broadcast([P, 2, CH]),
                                        ALU.mult).then_inc(prod_ok, 1)
                added[0] += 1
                pool.wait_ge(prod_ok, added[0])
                first = nc.gpsimd.tensor_tensor(acc, ada_prod[:, 0], ada_prod[:, 1] if a % 4 == 0 else acc, ALU.add)
                if a % 4 == 0:
                    first.then_inc(ada_done, 2)
                else:
                    first.then_inc(ada_done, 1)
                    pool.wait_ge(ada_done, 2 * a + 1)
                    nc.gpsimd.tensor_tensor(acc, ada_prod[:, 1], acc, ALU.add).then_inc(ada_done, 1)

            norm(0)
            pool.wait_ge(ada_done, 24)
            side = [pool.dma_start(lam_v[:, n, :], v[0].partition_broadcast(P)) for n, v in enumerate((lq1, lk1, lq2, lk2))]
            side += [pool.dma_start(freq_row[:], inv_freq.partition_broadcast(P))]
            with nc.allow_non_contiguous_dma(reason="256 positions"):
                side += [pool.dma_start(pos_i[:], positions[0].rearrange("(t p) -> p t", p=P))]
            side += [pool.dma_start(rope_a_sb[:], rope_a.rearrange("(t p) a r -> p t a r", p=P))]
            for load in side:
                load.then_inc(side_in, 16)
            for a in range(28, 36):
                fold(a)
            for first, end in HEADS_A:
                pool.wait_ge(o_sq, end)
                inv_sqrt(2 * first, 2 * (end - first), P).then_inc(qk_r, 1)
            norm(1)
            pool.wait_ge(mm_done, QKV_B)
            pool.dma_start(rope_b_sb[:], rope_b.rearrange("(t p) a d -> p t a d", p=P)).then_inc(late_in[0], 16)
            pool.dma_start(gain_b[:, 0, :], qnorm_g[0].partition_broadcast(P)).then_inc(late_in[0], 16)
            pool.dma_start(gain_b[:, 1, :], knorm_g[0].partition_broadcast(P)).then_inc(late_in[0], 16)
            norm(2)
            for a in range(76, 79):
                fold(a)
            pool.wait_ge(qk_sq0, 1)
            pool.wait_ge(qk_sq1, 1)
            inv_sqrt(16, 4, P).then_inc(qk_r, 1)
            for a in range(79, 82):
                fold(a)
            for half_ in range(2):
                pool.wait_ge(qk_sq0, 2 + half_)
                pool.wait_ge(qk_sq1, 2 + half_)
                inv_sqrt(8 * half_, 8, P).then_inc(qk_r, 1)
                fold(82 + half_)
            norm(3)
            pool.wait_ge(t_done, 4 * 6)
            pool.dma_start(row[:], final_g.partition_broadcast(P)).then_inc(late_in[1], 16)
            pool.wait_ge(mm_done, IN_C)
            pool.dma_start(mask_sb[:], masks).then_inc(late_in[2], 16)
            pool.dma_start(gmlp_row[:], gmlp_g[0].partition_broadcast(P)).then_inc(late_in[2], 16)
            norm(4)
            norm(5)
            pool.wait_ge(gm_sq, 1)
            inv_sqrt(0, 2, 768).then_inc(gm_r, 1)
            norm(6)
            pool.wait_ge(t_done, 4 * 10)
            pool.dma_start(row[:], final_g_c.partition_broadcast(P)).then_inc(late_in[3], 16)
            norm(7)

        AFFINE = {0: 0, 2: 1, 3: 2, 5: 3, 6: 4, 9: 5}

        @block.scalar
        def _(act):
            def split(m, turn=None):
                if m >= END:
                    return
                act.wait_ge(raw_in[m % RAW], at(32 * (m // RAW + 1), turn, 32))
                if m >= SPL:
                    act.wait_ge(mm_done, at(m - SPL + 1, turn, LOOP))
                nc.scalar.activation(w_hi[:, m % SPL], raw[:, m % RAW], ACT.Copy).then_inc(hi_done, 1)

            def square_0(n):
                if n == 0:
                    act.wait_ge(x_load, 16 * T)
                else:
                    act.wait_ge(x_ok, 2 * n - 1)
                nc.scalar.activation(xn[:, 0], x[:, 0], ACT.Square, accum_out=stat[:, SS:SS + 1]).then_inc(sq0, 1)

            def scale_0(n):
                act.wait_ge(rstd_ok, 2 * n + 1)
                nc.scalar.activation(xn[:, 0], x[:, 0], ACT.Copy, scale=stat[:, RSTD:RSTD + 1]).then_inc(xn0, 1)

            def operand(v, column=None):
                for kk in range(4):
                    if v in AFFINE:
                        act.wait_ge(hf_ok, 4 * AFFINE[v] + kk + 1)
                        nc.scalar.activation(h_hi[:, 2 * kk:2 * kk + 2], hf[:, 2 * kk:2 * kk + 2], ACT.Copy).then_inc(h_hi_ok, 1)
                    else:
                        act.wait_ge(t_done, 4 * v + kk + 1)
                        nc.scalar.activation(h_hi[:, 2 * kk:2 * kk + 2], bank[4 + kk][:].rearrange("p (k s) -> p k s", k=2),
                                             ACT.Copy, scale=1.0 if column is None else column).then_inc(h_hi_ok, 1)

            def take_chunk(base, done, c, b, turn=None):
                act.wait_ge(mm_done, at(base + 4 * (c + 1), turn, LOOP))
                for t in range(T):
                    last = nc.scalar.activation(proj[:, t, cols(c * CH, turn, 2 * CH, CH)], bank[2 * b + t][:], ACT.Copy)
                last.then_inc(evac, 1)

            def gate_half(n, h):
                act.wait_ge(gate_mm, 2 * n + h + 1)
                nc.scalar.activation(gate_row[:, h * CH:(h + 1) * CH], bank[7][:], ACT.Copy).then_inc(gate_ok, 1)

            def gate(n):
                gate_half(n, 0)
                gate_half(n, 1)

            act.wait_ge(const_ok, 3)
            nc.scalar.activation(stat[:, MISC + 7:MISC + 8], ones[:, 0:1], ACT.Silu)
            act.wait_ge(setup_t, 1)
            nc.scalar.activation(cond[:], bank[5][:, 0:KD], ACT.Silu).then_inc(setup, 1)
            for n, (src, first, rows, group) in enumerate((
                    (norm1_g[0], 0, 8, 0), (norm1_g[1], 8, 8, 0), (norm2_g[0], 16, 8, 0), (norm2_g[1], 24, 8, 0),
                    (mix_g[0], 32, 8, 0), (ffn_g_c[0], 40, 8, 0), (subln_g[0], 48, 1, 0))):
                act.dma_start(stage_v[first:first + rows, group, :], src.rearrange("(k p) -> k p", p=P)).then_inc(vec_in, 16)
            act.dma_start(stage_v[49:53, 0, :], b_spatial[0]).then_inc(vec_in, 16)
            act.dma_start(stage_v[0:96, 2, :], ada_b.rearrange("l (k p) -> (l k) p", p=P)).then_inc(vec_in, 16)
            act.dma_start(stage_v[0:3 * KF, 1, :], conv_w[0].rearrange("j (k p) -> (j k) p", p=P)).then_inc(vec_in, 16)
            act.dma_start(stage_v[3 * KF:4 * KF, 1, :], conv_b[0].rearrange("(k p) -> k p", p=P)).then_inc(vec_in, 16)
            square_0(0)
            act.wait_ge(setup_t, 2)
            nc.scalar.activation(vecs[:], bank[7][:, 0:237], ACT.Copy).then_inc(setup, 1)
            scale_0(0)
            act.wait_ge(setup_t, 3)
            nc.scalar.activation(w_spT[:], bank[6][:].rearrange("p (g t) -> p g t", g=4), ACT.Copy).then_inc(setup, 1)
            for m in range(SPL):
                split(m)
            operand(0)
            act.wait_ge(setup_v, 1)
            nc.scalar.activation(stat[:, MISC + 4:MISC + 6], stat[:, MISC + 2:MISC + 4], ACT.Exp).then_inc(setup, 1)
            with act.Fori(0, 2) as turn:
                for j in range(LOOP):
                    split(QKV_A + SPL + j, turn)
                    if j % 4 == 3:
                        take_chunk(QKV_A, 0, j // 4, j // 4, turn)
            for m in range(16, 24):
                if m in QK_STEPS_A:
                    n = 2 * (m - QK_STEPS_A[0]) + 1
                    f = QK_ORDER_A[n]
                    act.wait_ge(qk_t, n + 1)
                    nc.scalar.activation(qkT[:, 2 * f:2 * f + 2], bank[4 + n % 4][:].rearrange("p (k s) -> p k s", k=2),
                                         ACT.Copy).then_inc(qk_a, 1)
                split(QKV_A + SPL + m)
                if m % 4 == 3:
                    take_chunk(QKV_A, 0, m // 4, m // 4 % 2)
            NH = 8
            for i in range(NH + 3):
                if i < NH:
                    act.wait_ge(nmx_ok, i + 1)
                    for c in range(2):
                        for t in range(T):
                            n = 4 * i + 2 * c + t
                            last = nc.scalar.activation(
                                prob_a[:, i % 2, c, t], bank[2 * (i % 2) + c][:, t * S:(t + 1) * S], ACT.Exp,
                                bias=stat[:, NMX + n:NMX + n + 1], scale=0.125, accum_out=stat[:, DEN + n:DEN + n + 1])
                    last.then_inc(exp_ok, 1)
                if i in (1, 2):
                    gate_half(0, i - 1)
                if 2 <= i < NH + 2:
                    h = i - 2
                    act.wait_ge(wgt_t, h + 1)
                    nc.scalar.activation(wgtT[:, h % 2], bank[4 + h % 2][:].rearrange("p (k s) -> p k s", k=2),
                                         ACT.Copy).then_inc(wgt_ev, 1)
                if i >= 3:
                    h = i - 3
                    act.wait_ge(pv_ok, h + 1)
                    for t in range(T):
                        last = nc.scalar.activation(att[:, t, h * P:(h + 1) * P], bank[6 + h % 2][:, t * P:(t + 1) * P],
                                                    ACT.Square, scale=stat[:, RDEN + 4 * h + t:RDEN + 4 * h + t + 1],
                                                    accum_out=stat[:, SS + 2 * h + t:SS + 2 * h + t + 1])
                    last.then_inc(o_sq, 1)
            operand(1, column=stat[:, MISC + 6:MISC + 7])
            for m in range(WO_A, IN_0):
                split(m + SPL)
            square_0(1)
            scale_0(1)
            operand(2)

            def silu(base, f, c, b, turn=None):
                act.wait_ge(mm_done, at(base + 4 * (c + 1), turn, LOOP))
                for t in range(T):
                    last = nc.scalar.activation(act_s[:, b, t], bank[2 * b + t][:, 0:HC], ACT.Silu)
                last.then_inc(s_act, 1)

            def u_high(f, c, b, turn=None):
                act.wait_ge(u_t, at(NCH_FF * f + c + 1, turn, 2))
                nc.scalar.activation(u_hi[:, cols(2 * c, turn, 4, 2), :], bank[4 + b][:].rearrange("p (k s) -> p k s", k=2),
                                     ACT.Copy).then_inc(u_hi_ok, 1)

            def feed_forward(base, f, gate_n):
                for j in range(4):
                    split(base + SPL + j)
                silu(base, f, 0, 0)
                with act.Fori(0, 5) as turn:
                    for j in range(LOOP):
                        if j % 4 == 3:
                            u_high(f, j // 4, j // 4, turn)
                        split(base + 4 + SPL + j, turn)
                        if j % 4 == 3:
                            silu(base, f, 1 + j // 4, 1 - j // 4, turn)
                for k in range(KF):
                    if k == 3:
                        u_high(f, NCH_FF - 1, 0)
                    split(base + 4 * NCH_FF + SPL + k)
                    if k in (15, 18):
                        gate_half(gate_n, (k - 15) // 3)

            feed_forward(IN_0, 0, 1)
            square_0(2)
            scale_0(2)
            operand(3)
            def squares_b(h0, h1, part):
                act.wait_ge(evac, 7 + part)
                for h in range(h0, h1):
                    last = nc.scalar.activation(swap_b[:, 1, h], proj[:, 1, h * P:(h + 1) * P], ACT.Square,
                                                accum_out=stat[:, SS + 2 * h + 1:SS + 2 * h + 2])
                last.then_inc(qk_sq1, 1)

            def take_qk_b(n, b):
                f = (4, 0, 1, 2, 3)[n]
                act.wait_ge(qk_t, 8 + n + 1)
                nc.scalar.activation(qkT[:, 2 * f:2 * f + 2], bank[b][:].rearrange("p (k s) -> p k s", k=2),
                                     ACT.Copy).then_inc(qk_a, 1)

            for m in range(12):
                split(QKV_B + SPL + m)
                if m % 4 == 3:
                    act.wait_ge(mm_done, QKV_B + m + 1)
                    c = CHUNKS_B[m // 4]
                    for t in range(T):
                        last = nc.scalar.activation(proj[:, t, c * CH:(c + 1) * CH], bank[m // 4 % 2 * 2 + t][:], ACT.Copy)
                    last.then_inc(evac, 1)
                    if m == 11:
                        take_qk_b(1, 5)
                    squares_b(*((8, 10), (0, 4), (4, 8))[m // 4], m // 4)
                if m in (5, 10):
                    gate_half(2, (m - 5) // 5)
            for i in range(NH + 1):
                if i < NH:
                    act.wait_ge(nmx_ok, 8 + i + 1)
                    for t in range(T):
                        n = 2 * i + t
                        last = nc.scalar.activation(prob_b[:, i % 2, t], bank[i % 4][:, t * S:(t + 1) * S], ACT.Exp,
                                                    bias=stat[:, NMX + n:NMX + n + 1], scale=stat[:, RDEN + n:RDEN + n + 1],
                                                    accum_out=stat[:, DEN + n:DEN + n + 1])
                    last.then_inc(exp_ok, 1)
                if i >= 1:
                    h = i - 1
                    act.wait_ge(wgt_t, 8 + h + 1)
                    nc.scalar.activation(probT_b[:, h % 2], bank[4 + h % 2][:].rearrange("p (k s) -> p k s", k=2),
                                         ACT.Copy).then_inc(wgt_ev, 1)
                if i == 3:
                    take_qk_b(3, 2)
            operand(4)
            for m in range(WO_B, IN_1):
                split(m + SPL)
            square_0(3)
            scale_0(3)
            operand(5)
            act.wait_ge(setup_v, 2)
            nc.scalar.activation(ang_r[:], ang_r[:], ACT.Sin).then_inc(setup, 1)
            feed_forward(IN_1, 1, 3)
            square_0(4)
            square_0(5)
            scale_0(5)
            operand(6)
            with act.Fori(0, 2) as turn:
                for j in range(LOOP):
                    split(IN_C + SPL + j, turn)
                    if j % 4 == 3:
                        take_chunk(IN_C, 9, j // 4, j // 4, turn)
            act.wait_ge(evac, 9 + 4)
            for t in range(T):
                last = nc.scalar.activation(proj[:, t, 0:1536], proj[:, t, 0:1536], ACT.Gelu)
            last.then_inc(gelu_z, 1)
            act.wait_ge(gelu_z, 1)
            for t in range(T):
                last = nc.scalar.activation(rope_tc[:].rearrange("p a b c -> p (a b c)"), proj[:, t, 768:1536], ACT.Square,
                                            accum_out=stat[:, SS + t:SS + t + 1])
                if t == 0:
                    last.then_inc(gelu_z, 1)
                    act.wait_ge(gelu_z, 2)
            last.then_inc(gm_sq, 1)

            def c_exp_of(i):
                act.wait_ge(c_sm, i + 1)
                for t, (first, width) in enumerate(((0, 384), (384, 768))):
                    n = 2 * i + t
                    part = prob_c[:, i % 2, first:first + width]
                    last = nc.scalar.activation(part, part, ACT.Exp, bias=stat[:, NMX + n:NMX + n + 1],
                                                accum_out=stat[:, DEN + n:DEN + n + 1])
                last.then_inc(c_exp, 1)

            def take_probT(i):
                act.wait_ge(c_pt, i + 1)
                if i >= 1:
                    act.wait_ge(c_pv, i)
                for q, (first, n) in enumerate(((0, 4), (4, 4), (8, 1))):
                    last = nc.scalar.activation(probT_c[:, first:first + n], bank[5 + q][:, 0:n * P].rearrange(
                        "p (k s) -> p k s", k=n), ACT.Copy)
                last.then_inc(c_pev, 1)

            for m in range(16, 46):
                if m in QK_STEPS:
                    f = 2 * (m - QK_STEPS[0]) + 1
                    act.wait_ge(c_qkt, f + 1)
                    nc.scalar.activation(qkT[:, 2 * f:2 * f + 2], bank[4 + f % 4][:].rearrange("p (k s) -> p k s", k=2),
                                         ACT.Copy).then_inc(c_qka, 1)
                if m - 1 in SCORE_STEPS:
                    c_exp_of(SCORE_STEPS.index(m - 1))
                if m in PROBT_STEPS:
                    take_probT(PROBT_STEPS.index(m))
                split(IN_C + SPL + m)
                if m == 22:
                    act.wait_ge(gm_r, 1)
                    for t in range(T):
                        last = nc.scalar.activation(proj[:, t, 768:1536], proj[:, t, 768:1536], ACT.Copy,
                                                    scale=stat[:, RSTD + t:RSTD + t + 1])
                    last.then_inc(gm_v, 1)
                if m < 44 and m % 4 == 3:
                    take_chunk(IN_C, 9, m // 4, c_bank(m // 4))
            act.wait_ge(mm_done, TAIL_C + 2)
            for t in range(T):
                last = nc.scalar.activation(proj[:, t, 11 * CH:W2_COLS], bank[t][:, 0:HC], ACT.Copy)
            last.then_inc(evac, 1)
            operand(7)
            for m in range(BR_A, OUT_C):
                split(m + SPL)
                if m == BR_A + 1:
                    act.wait_ge(evac, 9 + 12)
                    for t in range(T):
                        last = nc.scalar.activation(proj[:, t, 3840:W2_COLS], proj[:, t, 3840:W2_COLS], ACT.Sigmoid)
                    last.then_inc(sig_g, 1)
            operand(8)
            for m in range(OUT_C, UP_C):
                split(m + SPL)
            square_0(6)
            scale_0(6)
            operand(9)

            def take_pair(c, b, turn=None):
                act.wait_ge(mm_done, at(UP_C + 4 * (c + 1), turn, LOOP))
                for t in range(T):
                    last = nc.scalar.activation(av[:, b, t], bank[2 * b + t][:], ACT.Copy)
                last.then_inc(av_ok, 1)

            def gelu(c, b, turn=None):
                act.wait_ge(conv_ok, at(c + 1, turn, 2))
                nc.scalar.activation(conv_t[:, b], conv_t[:, b], ACT.Gelu).then_inc(gelu_ok, 1)

            def c_high(c, b, turn=None):
                act.wait_ge(cu_ok, at(c + 1, turn, 2))
                nc.scalar.activation(u_hi[:, cols(2 * c, turn, 4, 2), :], conv_t[:, b], ACT.Copy).then_inc(c_hi, 1)

            nc.scalar.activation(stat[:, MISC + 7:MISC + 8], stat[:, SS:SS + 1], ACT.Gelu)
            for j in range(4):
                split(UP_C + SPL + j)
            take_pair(0, 0)
            with act.Fori(0, 5) as turn:
                for j in range(LOOP):
                    split(UP_C + 4 + SPL + j, turn)
                    if j % 4 == 3:
                        take_pair(1 + j // 4, 1 - j // 4, turn)
                        gelu(j // 4, j // 4, turn)
                        c_high(j // 4, j // 4, turn)
            for k in range(KF):
                if k == 3:
                    gelu(NCH_FF - 1, 0)
                split(DOWN_C + SPL + k)
                if k == 3:
                    c_high(NCH_FF - 1, 0)
            square_0(7)

        @block.vector
        def _(v_):
            ve = nc.vector
            chain = [0]

            def link(ins):
                chain[0] += 1
                ins.then_inc(dve, 1)
                v_.wait_ge(dve, chain[0])

            def low(m, turn=None):
                if m >= END:
                    return
                v_.wait_ge(hi_done, at(m + 1, turn, LOOP))
                ve.tensor_tensor(w_lo[:, m % SPL], raw[:, m % RAW], w_hi[:, m % SPL].bitcast(F32),
                                 ALU.subtract).then_inc(lo_done, 1)

            def fold(a, turn=None):
                g, u = divmod(a, 4)
                v_.wait_ge(ada_in[a % ADA_SLOTS], at(16 * (a // ADA_SLOTS + 1), turn, 16))
                acc = ada_acc[:, acc_slot(g)]
                for k in range(2):
                    n = 2 * a + k
                    w = ada[:, a % ADA_SLOTS, k]
                    if n % 8 == 0:
                        if g >= 2:
                            v_.wait_ge(ada_red, at(last_in_slot(g) + 1, turn, 1))
                        if n:
                            v_.wait_ge(ada_done, at(n, turn, 8))
                        ve.tensor_scalar(acc, w, cond[:, 0:1], None, ALU.mult).then_inc(ada_done, 1)
                    else:
                        v_.wait_ge(ada_done, at(n, turn, 8))
                        ve.scalar_tensor_tensor(out=acc, in0=w, scalar=cond[:, n % 8:n % 8 + 1], in1=acc, op0=ALU.mult, op1=ALU.add).then_inc(ada_done, 1)

            def take_group(g, turn=None):
                v_.wait_ge(ada_red, at(g + 1, turn, 1))
                ve.tensor_tensor(mod[:, cols(4 * g, turn, 4, 4)], bank[sum_bank(g)][:, 0:4],
                                 vecs[:, cols(ADAB_V + 4 * g, turn, 4, 4)], ALU.add).then_inc(ada_col, 1)

            def fold_step(g, j, turn=None, steps=LOOP_FOLD, takes=LOOP_TAKE):
                if j in takes:
                    take_group(g + takes[j], turn)
                if j in steps:
                    fold(4 * g + steps[j], turn)

            def square_1(n):
                if n == 0:
                    v_.wait_ge(x_load, 16 * T)
                ve.tensor_tensor_reduce(out=xn[:, 1], in0=x[:, 1], in1=x[:, 1], scale=1.0, scalar=0.0, op0=ALU.mult,
                                        op1=ALU.add, accum_out=stat[:, SS + 1:SS + 2]).then_inc(sq1, 1)

            def scale_1(n):
                v_.wait_ge(rstd_ok, 2 * n + 2)
                ve.tensor_scalar(xn[:, 1], x[:, 1], stat[:, RSTD + 1:RSTD + 2], None, ALU.mult).then_inc(xn1, 1)

            def make_gains(first, group):
                v_.wait_ge(ada_col, group)
                link(ve.scalar_tensor_tensor(out=gains[:], in0=mod[:, 4 * (group - 2):4 * group], scalar=1.0,
                                             in1=vecs[:, first:first + KD], op0=ALU.add, op1=ALU.mult))

            def operand(v, gain=None, shift=None, column=None, then=None):
                def affine(kk):
                    v_.wait_ge(t_done, 4 * v + kk + 1)
                    for k in (2 * kk, 2 * kk + 1):
                        last = ve.tensor_scalar(hf[:, k], bank[4 + kk][:, k % 2 * S:(k % 2 + 1) * S], gain[:, k:k + 1],
                                                0.0 if shift is None else shift[:, k:k + 1], ALU.mult, ALU.add)
                    last.then_inc(hf_ok, 1)

                for kk in range(4):
                    if v in AFFINE:
                        if kk == 0:
                            affine(0)
                        if kk < 3:
                            affine(kk + 1)
                        v_.wait_ge(hf_ok, 4 * AFFINE[v] + kk + 1)
                    v_.wait_ge(h_hi_ok, 4 * v + kk + 1)
                    out_, hi = h_lo[:, 2 * kk:2 * kk + 2], h_hi[:, 2 * kk:2 * kk + 2].bitcast(F32)
                    ps = bank[4 + kk][:].rearrange("p (k s) -> p k s", k=2)
                    if v in AFFINE:
                        last = ve.tensor_tensor(out_, hf[:, 2 * kk:2 * kk + 2], hi, ALU.subtract)
                    elif column is None:
                        last = ve.tensor_tensor(out_, ps, hi, ALU.subtract)
                    else:
                        last = ve.scalar_tensor_tensor(out=out_, in0=ps, scalar=column, in1=hi, op0=ALU.mult,
                                                       op1=ALU.subtract)
                    last.then_inc(h_lo_ok, 1)
                    if then is not None:
                        then(kk)

            def gate(n, first, h):
                if 2 * n + h:
                    v_.wait_ge(gate_mm, 2 * n + h)
                c0 = first + 4 * h
                ve.tensor_tensor(diag[:], ident[:].unsqueeze(1).to_broadcast([P, 4, P]),
                                 mod[:, c0:c0 + 4].unsqueeze(2).to_broadcast([P, 4, P]), ALU.mult).then_inc(gate_diag, 1)

            def residual(done, gated):
                v_.wait_ge(mm_done, done)
                if gated is not None:
                    v_.wait_ge(gate_ok, 2 * gated + 2)

                    def product(t, n):
                        gated_done[0] += 1
                        ve.tensor_tensor(res[:, 2 * t + n], bank[2 * n + t][:], gate_row[:, n * CH:(n + 1) * CH],
                                         ALU.mult).then_inc(res_ok, 1)

                    product(0, 0)
                    product(0, 1)
                for t in range(T):
                    if gated is not None:
                        ready = gated_done[0]
                        if t == 0:
                            product(1, 0)
                        v_.wait_ge(res_ok, ready)
                        ve.tensor_tensor(x[:, t], x[:, t], res[:, 2 * t:2 * t + 2].rearrange("p n c -> p (n c)"),
                                         ALU.add).then_inc(x_ok, 1)
                        if t == 0:
                            product(1, 1)
                    else:
                        for n in range(2):
                            part = x[:, t, n * CH:(n + 1) * CH]
                            last = ve.tensor_tensor(part, bank[2 * n + t][:], part, ALU.add)
                        last.then_inc(x_ok, 1)
                residuals[0] += 1
                v_.wait_ge(x_ok, 2 * residuals[0])

            gated_done = [0]
            residuals = [0]
            v_.wait_ge(setup, 1)
            for a in range(16):
                fold(a)
                if a == 7:
                    square_1(0)
                if a == 9:
                    scale_1(0)
                if a in (8, 10, 13):
                    if a == 8:
                        v_.wait_ge(setup, 2)
                    take_group((8, 10, 13).index(a))
            low(0)
            take_group(3)
            make_gains(N1_V, 4)
            def minus_lambda():
                v_.wait_ge(side_in, 16 * SIDE)
                for n in range(2):
                    ins = ve.tensor_tensor_reduce(out=lam_v[:, 2 * n], in0=lam_v[:, 2 * n], in1=lam_v[:, 2 * n + 1], scale=1.0,
                                                  scalar=0.0, op0=ALU.mult, op1=ALU.add,
                                                  accum_out=stat[:, MISC + 2 + n:MISC + 3 + n])
                ins.then_inc(setup_v, 1)
                v_.wait_ge(setup, 4)
                link(ve.tensor_tensor(neg_lam, stat[:, MISC + 5:MISC + 6], stat[:, MISC + 4:MISC + 5], ALU.subtract))
                link(ve.tensor_scalar(neg_lam, neg_lam, LAM_INIT, None, ALU.subtract))
                link(ve.tensor_scalar(stat[:, MISC + 6:MISC + 7], vecs[:, SUB_V:SUB_V + 1], 1.0 - LAM_INIT, None, ALU.mult))

            def angles():
                link(ve.tensor_copy(pos_f[:], pos_i[:]))
                link(ve.tensor_tensor(ang[:], pos_f[:].unsqueeze(2).to_broadcast([P, T, 8]),
                                      freq_row[:].unsqueeze(1).to_broadcast([P, T, 8]), ALU.mult))
                hi = 6.28125
                mid = float(np.float32(TWO_PI - hi)) // 2.0 ** -19 * 2.0 ** -19
                lo = TWO_PI - hi - mid
                for q, quarter in enumerate((math.pi / 2, 0.0)):
                    n, r = ang_n[:, :, q], ang_r[:, :, q]
                    link(ve.tensor_scalar(n, ang[:], 1 / TWO_PI, quarter / TWO_PI, ALU.mult, ALU.add))
                    link(ve.tensor_scalar(n, n, ROUND, None, ALU.add))
                    link(ve.tensor_scalar(n, n, ROUND, None, ALU.subtract))
                    link(ve.scalar_tensor_tensor(out=r, in0=n, scalar=-hi, in1=ang[:], op0=ALU.mult, op1=ALU.add))
                    link(ve.scalar_tensor_tensor(out=r, in0=n, scalar=-mid, in1=r, op0=ALU.mult, op1=ALU.add))
                    link(ve.scalar_tensor_tensor(out=r, in0=n, scalar=-lo, in1=r, op0=ALU.mult, op1=ALU.add))
                    link(ve.tensor_scalar(r, r, quarter, None, ALU.add))
                    link(ve.tensor_scalar(r, r, PI_IN, -PI_IN, ALU.min, ALU.max))
                ve.tensor_copy(stat[:, MISC + 7:MISC + 8], stat[:, MISC + 2:MISC + 3]).then_inc(setup_v, 1)
                v_.wait_ge(setup, 5)
                for h in range(2):
                    ve.tensor_copy(rope_c_sb[:, :, 0, 8 * h:8 * h + 8], ang_r[:, :, 0])
                ve.tensor_scalar(rope_c_sb[:, :, 1, 0:8], ang_r[:, :, 1], -1.0, None, ALU.mult)
                link(ve.tensor_copy(rope_c_sb[:, :, 1, 8:16], ang_r[:, :, 1]))

            PI_IN = float(np.nextafter(np.float32(math.pi), np.float32(0)))
            operand(0, gains[:], mod[:, 0:8], then=lambda kk: kk < 3 and low(kk + 1))
            minus_lambda()
            with v_.Fori(0, 2) as turn:
                for j in range(LOOP):
                    low(QKV_A + SPL + j, turn)
                    fold_step(4, j, turn)

            def rotate(first, heads, table, tmp, need):
                v_.wait_ge(evac, need)
                q = proj[:, :, first:first + heads * 64].rearrange("p t (h d) -> p t h d", d=64)[:, :, :, 0:16]
                for h in range(2):
                    for t in range(T):
                        last = ve.tensor_tensor(
                            tmp[:, t, :, 8 * h:8 * h + 8], q[:, t, :, 8 - 8 * h:16 - 8 * h],
                            table[:, t, 1, 8 * h:8 * h + 8].unsqueeze(1).to_broadcast([P, heads, 8]), ALU.mult)
                link(last)
                for t in range(T):
                    last = ve.tensor_tensor(q[:, t], q[:, t], table[:, t, 0].unsqueeze(1).to_broadcast([P, heads, 16]), ALU.mult)
                link(last)
                for t in range(T):
                    last = ve.tensor_tensor(q[:, t], q[:, t], tmp[:, t], ALU.add)
                last.then_inc(rope_ok, 1)

            for m in range(16, 24):
                if m == 16:
                    rotate(0, 32, rope_a_sb, rope_t, 4)
                if m in QK_STEPS_A:
                    n = 2 * (m - QK_STEPS_A[0])
                    f = QK_ORDER_A[n]
                    v_.wait_ge(qk_t, n + 1)
                    ve.tensor_copy(qkT[:, 2 * f:2 * f + 2], bank[4 + n % 4][:].rearrange("p (k s) -> p k s", k=2)).then_inc(qk_d, 1)
                low(QKV_A + SPL + m)
                fold_step(6, m - 16)
            NH = 8
            def scale_heads(part):
                first, end = HEADS_A[part]
                v_.wait_ge(o_ok, end)
                v_.wait_ge(qk_r, part + 1)
                for t in range(T):
                    o = att[:, t, first * P:end * P].rearrange("p (h e) -> p h e", e=P)
                    r = stat[:, RSTD + 2 * first:RSTD + 2 * end].rearrange("p (h t) -> p t h", t=2)[:, t]
                    last = ve.tensor_tensor(o, o, r.unsqueeze(2).to_broadcast([P, end - first, P]), ALU.mult)
                    if part == 2:
                        last.then_inc((xn0, xn1)[t], 1)

            for i in range(NH + 4):
                if i < NH:
                    v_.wait_ge(sc_ok, i + 1)
                    for c in range(2):
                        n = MX + 4 * i + 2 * c
                        last = ve.tensor_reduce(stat[:, n:n + 2], bank[2 * (i % 2) + c][:].rearrange("p (t s) -> p t s", t=2),
                                                AX.X, ALU.max)
                    link(last)
                    ve.tensor_scalar(stat[:, NMX + 4 * i:NMX + 4 * i + 4], stat[:, MX + 4 * i:MX + 4 * i + 4], -0.125, None,
                                     ALU.mult).then_inc(nmx_ok, 1)
                if i < 2:
                    gate(0, 16, i)
                if 1 <= i <= NH:
                    h = i - 1
                    v_.wait_ge(exp_ok, h + 1)
                    r = stat[:, RDEN + 4 * h:RDEN + 4 * h + 4]
                    link(ve.reciprocal(r, stat[:, DEN + 4 * h:DEN + 4 * h + 4]))
                    link(ve.scalar_tensor_tensor(out=r[:, 2:4], in0=r[:, 2:4], scalar=neg_lam, in1=stat[:, DEN + 4 * h:DEN + 4 * h + 2],
                                                 op0=ALU.mult, op1=ALU.mult))
                    if h >= 2:
                        v_.wait_ge(wgt_t, h - 1)
                    for t in range(T):
                        last = ve.scalar_tensor_tensor(out=wgt[:, h % 2, t], in0=prob_a[:, h % 2, 1, t], scalar=r[:, 2 + t:3 + t],
                                                       in1=prob_a[:, h % 2, 0, t], op0=ALU.mult, op1=ALU.add)
                    last.then_inc(wgt_ok, 1)
                if i >= 4:
                    h = i - 4
                    if h in (5, 7):
                        scale_heads((h - 5) // 2)
                    v_.wait_ge(o_sq, h + 1)
                    for t in range(T):
                        last = ve.tensor_scalar(att[:, t, h * P:(h + 1) * P], bank[6 + h % 2][:, t * P:(t + 1) * P],
                                                stat[:, RDEN + 4 * h + t:RDEN + 4 * h + t + 1], None, ALU.mult)
                    last.then_inc(o_ok, 1)
            scale_heads(2)
            operand(1, column=stat[:, MISC + 6:MISC + 7])
            for m in range(WO_A, IN_0):
                if m < IN_0 - 1:
                    low(m + SPL)
                k = m - WO_A
                fold_step(7, k, steps={2: 8, 3: 9, 4: 10, 5: 11}, takes={2: 0, 4: 1})
            residual(IN_0, 0)
            square_1(1)
            take_group(9)
            make_gains(N2_V, 10)
            low(IN_0 + SPL - 1)
            scale_1(1)
            operand(2, gains[:], mod[:, 24:32])

            def glu(f, c, b, turn=None):
                v_.wait_ge(s_act, at(NCH_FF * f + c + 1, turn, 2))
                for t in range(T):
                    last = ve.tensor_tensor(act_u[:, b, t], bank[2 * b + t][:, HC:CH], act_s[:, b, t], ALU.mult)
                last.then_inc(u_ok, 1)

            def u_low(f, c, b, turn=None):
                v_.wait_ge(u_hi_ok, at(NCH_FF * f + c + 1, turn, 2))
                ve.tensor_tensor(u_lo[:, cols(2 * c, turn, 4, 2), :], bank[4 + b][:].rearrange("p (k s) -> p k s", k=2),
                                 u_hi[:, cols(2 * c, turn, 4, 2), :].bitcast(F32), ALU.subtract).then_inc(u_lo_ok, 1)

            def feed_forward(base, f, gate_n, gate_c, with_ada, out_g, out_n):
                for j in range(4):
                    low(base + SPL + j)
                glu(f, 0, 0)
                with v_.Fori(0, 5) as turn:
                    for j in range(LOOP):
                        if j % 4 == 3:
                            u_low(f, j // 4, j // 4, turn)
                        low(base + 4 + SPL + j, turn)
                        if with_ada:
                            fold_step(10, j, turn)
                        if j % 4 == 3:
                            glu(f, 1 + j // 4, 1 - j // 4, turn)
                for k in range(KF):
                    if k == 3:
                        u_low(f, NCH_FF - 1, 0)
                    if k < KF - 1:
                        low(base + 4 * NCH_FF + SPL + k)
                    fold_step(out_g, k, steps=first_steps(OUT_FOLD, 4 * out_n), takes=first_steps(OUT_TAKE, out_n))
                    if k in (12, 15):
                        gate(gate_n, gate_c, (k - 12) // 3)
                residual(base + 4 * NCH_FF + KF, gate_n)

            feed_forward(IN_0, 0, 1, 40, True, 15, 4)
            square_1(2)
            make_gains(N1_V + KD, 16)
            low(QKV_B + SPL - 1)
            scale_1(2)
            operand(3, gains[:], mod[:, 48:56])
            def table():
                v_.wait_ge(late_in[0], 48)
                for a in range(2):
                    for t in range(T):
                        ve.tensor_tensor(table_b[:, t, a, 0], rope_b_sb[:, t, 0], gain_b[:, a], ALU.mult)
                        for lo, hi in ((0, 32), (32, 0), (64, 96), (96, 64)):
                            last = ve.tensor_tensor(table_b[:, t, a, 1, lo:lo + 32], rope_b_sb[:, t, 1, lo:lo + 32],
                                                    gain_b[:, a, hi:hi + 32], ALU.mult)
                link(last)

            def square_and_swap(h0, h1, a, part):
                v_.wait_ge(evac, 7 + part)
                q = proj[:, 0, h0 * P:h1 * P].rearrange("p (h d) -> p h d", d=P)
                link(ve.tensor_tensor(swap_b[:, 0, h0:h1], q, q, ALU.mult))
                ve.tensor_reduce(stat[:, SS:SS + 20].rearrange("p (h t) -> p t h", t=2)[:, 0, h0:h1], swap_b[:, 0, h0:h1],
                                 AX.X, ALU.add).then_inc(qk_sq0, 1)
                v_.wait_ge(qk_sq0, part + 1)
                v_.wait_ge(qk_sq1, part + 1)
                for t in range(T):
                    q = proj[:, t, h0 * P:h1 * P].rearrange("p (h q e r) -> p h q e r", q=2, e=2, r=32)
                    sw = swap_b[:, t, h0:h1].rearrange("p h (q e r) -> p h q e r", q=2, e=2)
                    tab = table_b[:, t, a, 1].rearrange("p (q e r) -> p q e r", q=2, e=2)
                    for e in range(2):
                        for qq in range(2):
                            last = ve.tensor_tensor(sw[:, :, qq, e], q[:, :, qq, 1 - e],
                                                    tab[:, qq, e].unsqueeze(1).to_broadcast([P, h1 - h0, 32]), ALU.mult)
                link(last)

            def turn(h0, h1, a, part):
                for t in range(T):
                    q = proj[:, t, h0 * P:h1 * P].rearrange("p (h d) -> p h d", d=P)
                    last = ve.tensor_tensor(q, q, table_b[:, t, a, 0].unsqueeze(1).to_broadcast([P, h1 - h0, P]), ALU.mult)
                link(last)
                for t in range(T):
                    q = proj[:, t, h0 * P:h1 * P].rearrange("p (h d) -> p h d", d=P)
                    last = ve.tensor_tensor(q, q, swap_b[:, t, h0:h1], ALU.add)
                if part == 0:
                    link(last)
                else:
                    last.then_inc(rope_ok, 1)

            def scale_keys():
                v_.wait_ge(qk_r, 4)
                for t in range(T):
                    k = proj[:, t, 1024:1280].rearrange("p (h d) -> p h d", d=P)
                    r = stat[:, RSTD + 16:RSTD + 20].rearrange("p (h t) -> p t h", t=2)[:, t]
                    last = ve.tensor_tensor(k, k, r.unsqueeze(2).to_broadcast([P, 2, P]), ALU.mult)
                last.then_inc(rope_ok, 1)

            def query_scales(part):
                v_.wait_ge(qk_r, 4 + part)
                first = 8 * (part - 1)
                link(ve.tensor_scalar(stat[:, RDEN + first:RDEN + first + 8], stat[:, RSTD + first:RSTD + first + 8], P ** -0.5,
                                      None, ALU.mult))

            def take_qk_b(n, b):
                f = (4, 0, 1, 2, 3)[n]
                v_.wait_ge(qk_t, 8 + n + 1)
                ve.tensor_copy(qkT[:, 2 * f:2 * f + 2], bank[b][:].rearrange("p (k s) -> p k s", k=2)).then_inc(qk_d, 1)

            for m in range(12):
                if m == 1:
                    table()
                if m == K_STEP_B:
                    square_and_swap(8, 10, 1, 0)
                    turn(8, 10, 1, 0)
                if m == K_SCALE_STEP_B:
                    scale_keys()
                if m == Q_STEP_B:
                    square_and_swap(0, 4, 0, 1)
                if m == Q_STEP_B + 1:
                    turn(0, 4, 0, 1)
                if m == K_TURN_STEP_B + 2:
                    take_qk_b(0, 4)
                low(QKV_B + SPL + m)
                fold_step(19, m, steps={}, takes=B_TAKE)
                if m in (2, 7):
                    gate(2, 64, (m - 2) // 5)
            take_qk_b(2, 6)
            query_scales(1)

            def max_b(i):
                v_.wait_ge(sc_ok, 8 + i + 1)
                n = MX + 2 * i
                link(ve.tensor_reduce(stat[:, n:n + 2], bank[i % 4][:].rearrange("p (t s) -> p t s", t=2), AX.X, ALU.max))
                ve.scalar_tensor_tensor(out=stat[:, NMX + 2 * i:NMX + 2 * i + 2], in0=stat[:, n:n + 2], scalar=-1.0,
                                        in1=stat[:, RDEN + 2 * i:RDEN + 2 * i + 2], op0=ALU.mult,
                                        op1=ALU.mult).then_inc(nmx_ok, 1)

            def out_b(h):
                v_.wait_ge(pv_ok, 8 + h + 1)
                den = stat[:, DEN + 2 * h:DEN + 2 * h + 2]
                link(ve.reciprocal(den, den))
                for t in range(T):
                    last = ve.tensor_scalar(att_b[:, t, h * P:(h + 1) * P], bank[6 + h % 2][:, t * P:(t + 1) * P],
                                            den[:, t:t + 1], None, ALU.mult)
                    if h == NH - 1:
                        last.then_inc((xn0, xn1)[t], 1)
                if h < NH - 1:
                    last.then_inc(o_ok, 1)

            for i in range(NH + 2):
                if i == 2:
                    square_and_swap(4, 8, 0, 2)
                if i == 4:
                    turn(4, 8, 0, 2)
                    query_scales(2)
                    out_b(0)
                    take_qk_b(4, 3)
                    out_b(1)
                if i < NH:
                    max_b(i)
                if i >= 4:
                    out_b(i - 2)
            operand(4)
            for m in range(WO_B, IN_1):
                if m < IN_1 - 1:
                    low(m + SPL)
                fold_step(20, m - WO_B, steps={1: 4, 2: 5, 3: 6, 4: 7}, takes={3: 0, 7: 1})
            residual(IN_1, 2)
            square_1(3)
            make_gains(N2_V + KD, 22)
            low(IN_1 + SPL - 1)
            scale_1(3)
            operand(5, gains[:], mod[:, 72:80])
            angles()
            feed_forward(IN_1, 1, 3, 88, False, 22, 2)
            square_1(4)
            v_.wait_ge(late_in[1], 16)
            for t in range(T):
                v_.wait_ge(rstd_ok, 2 * 4 + t + 1)
                ve.scalar_tensor_tensor(out=x[:, t], in0=x[:, t], scalar=stat[:, RSTD + t:RSTD + t + 1], in1=row[:],
                                        op0=ALU.mult, op1=ALU.mult).then_inc(x_ok, 1)
            residuals[0] += 1
            v_.wait_ge(x_ok, 2 * residuals[0])
            square_1(5)
            low(IN_C + SPL - 1)
            scale_1(5)
            operand(6, vecs[:, MIX_V:MIX_V + KD])
            with v_.Fori(0, 3) as turn:
                for j in range(LOOP):
                    low(IN_C + SPL + j, turn)

            def spatial():
                v_.wait_ge(late_in[2], 32)
                v_.wait_ge(gm_mm, 1)
                for t in range(T):
                    for gp in range(2):
                        last = ve.tensor_tensor(y_c[:, t, 384 * gp:384 * gp + 384], bank[4 + 2 * t + gp][:, 0:384],
                                                gmlp_row[:, 384 * gp:384 * gp + 384], ALU.mult)
                last.then_inc(gm_y, 1)
                v_.wait_ge(gm_y, 1)
                for t in range(T):
                    for g in range(4):
                        y = y_c[:, t, 192 * g:192 * g + 192]
                        ve.scalar_tensor_tensor(out=y, in0=y, scalar=vecs[:, BSP_V + g:BSP_V + g + 1],
                                                in1=proj[:, t, 192 * g:192 * g + 192], op0=ALU.add, op1=ALU.mult)

            def mask_and_max(i):
                v_.wait_ge(c_sc, i + 1)
                if i >= 2:
                    v_.wait_ge(c_pt, i - 1)
                for t, (first, width) in enumerate(((0, P), (384, S))):
                    for g in range(3):
                        c0 = first + g * width
                        last = ve.scalar_tensor_tensor(out=prob_c[:, i % 2, c0:c0 + width], in0=bank[2 + g][:, t * S:t * S + width],
                                                       scalar=0.125, in1=mask_sb[:, c0:c0 + width], op0=ALU.mult, op1=ALU.add)
                link(last)
                for t, (first, width) in enumerate(((0, 384), (384, 768))):
                    n = MX + 2 * i + t
                    last = ve.tensor_reduce(stat[:, n:n + 1], prob_c[:, i % 2, first:first + width], AX.X, ALU.max)
                link(last)
                ve.tensor_scalar(stat[:, NMX + 2 * i:NMX + 2 * i + 2], stat[:, MX + 2 * i:MX + 2 * i + 2], -1.0, None,
                                 ALU.mult).then_inc(c_sm, 1)

            def head_out(h):
                v_.wait_ge(c_pv, h + 1)
                den = stat[:, DEN + 2 * h:DEN + 2 * h + 2]
                link(ve.reciprocal(den, den))
                for t in range(T):
                    last = ve.tensor_scalar(y_c[:, t, 768 + 64 * h:768 + 64 * h + 64], bank[7][:, 256 + t * 64:320 + t * 64],
                                            den[:, t:t + 1], None, ALU.mult)
                    if h == 3:
                        last.then_inc((xn0, xn1)[t], 1)
                if h < 3:
                    last.then_inc(c_o, 1)

            for m in range(24, 47):
                if m == 24:
                    rotate(1536, 24, rope_c_sb, rope_tc, 15)
                if m in QK_STEPS:
                    f = 2 * (m - QK_STEPS[0])
                    v_.wait_ge(c_qkt, f + 1)
                    ve.tensor_copy(qkT[:, 2 * f:2 * f + 2], bank[4 + f % 4][:].rearrange("p (k s) -> p k s", k=2)).then_inc(c_qkd, 1)
                if m == SPATIAL_STEP:
                    spatial()
                if m in SCORE_STEPS:
                    mask_and_max(SCORE_STEPS.index(m))
                if m in PV_STEPS:
                    head_out(PV_STEPS.index(m))
                if m < 46:
                    low(IN_C + SPL + m)
            operand(7)
            for m in range(BR_A, BR_B):
                low(m + SPL)
            v_.wait_ge(sig_g, 1)
            v_.wait_ge(mm_done, BR_B)
            for t in range(T):
                for n in range(2):
                    ve.tensor_tensor(merged[:, t, n * CH:(n + 1) * CH], bank[2 * n + t][:],
                                     proj[:, t, 3840 + n * CH:3840 + (n + 1) * CH], ALU.mult)
            low(BR_B + SPL)
            v_.wait_ge(mm_done, OUT_C)

            def second_branch(t, n):
                ve.tensor_tensor(merged_b[:, 2 * t + n], bank[4 + 2 * n + t][:],
                                 proj[:, t, 4864 + n * CH:4864 + (n + 1) * CH], ALU.mult).then_inc(br_ok, 1)

            second_branch(0, 0)
            second_branch(0, 1)
            for t in range(T):
                if t == 0:
                    second_branch(1, 0)
                v_.wait_ge(br_ok, 2 + 2 * t)
                m2 = merged[:, t]
                ve.tensor_tensor(m2, m2, merged_b[:, 2 * t:2 * t + 2].rearrange("p n c -> p (n c)"), ALU.add).then_inc(
                    (xn0, xn1)[t], 1)
                if t == 0:
                    second_branch(1, 1)
            low(BR_B + 1 + SPL)
            operand(8)
            for m in range(OUT_C, UP_C - 1):
                low(m + SPL)
            residual(UP_C, None)
            square_1(6)
            low(UP_C + SPL - 1)
            scale_1(6)
            operand(9, vecs[:, FFN_V:FFN_V + KD])

            def conv(c, b, turn=None):
                v_.wait_ge(av_t, at(c + 1, turn, 2))
                a = bank[4 + b][:].rearrange("p (k s) -> p k s", k=2)
                for tap in (2, 1, 0):
                    d = 2 - tap
                    for k in range(2):
                        w = vecs[:, cols(CONV_V + KF * tap + 2 * c + k, turn, 4, 1)]
                        o = conv_t[:, b, k]
                        if tap == 2:
                            last = ve.tensor_scalar(o, a[:, k], w, vecs[:, cols(CONV_V + KF * 3 + 2 * c + k, turn, 4, 1)],
                                                    ALU.mult, ALU.add)
                        else:
                            last = ve.scalar_tensor_tensor(out=o[:, d:S], in0=a[:, k, 0:S - d], scalar=w, in1=o[:, d:S],
                                                           op0=ALU.mult, op1=ALU.add)
                    if tap:
                        last.then_inc(dve_conv, 1)
                        v_.wait_ge(dve_conv, at(2 * c + d + 1, turn, 4))
                last.then_inc(conv_ok, 1)

            def conv_glu(c, b, turn=None):
                v_.wait_ge(gelu_ok, at(c + 1, turn, 2))
                ve.tensor_tensor(conv_t[:, b], bank[6 + b][:].rearrange("p (k s) -> p k s", k=2), conv_t[:, b],
                                 ALU.mult).then_inc(cu_ok, 1)

            def c_low(c, b, turn=None):
                v_.wait_ge(c_hi, at(c + 1, turn, 2))
                ve.tensor_tensor(u_lo[:, cols(2 * c, turn, 4, 2), :], conv_t[:, b],
                                 u_hi[:, cols(2 * c, turn, 4, 2), :].bitcast(F32), ALU.subtract).then_inc(c_lo, 1)

            for j in range(4):
                low(UP_C + SPL + j)
            with v_.Fori(0, 5) as turn:
                for j in range(LOOP):
                    low(UP_C + 4 + SPL + j, turn)
                    if j % 4 == 2:
                        conv(j // 4, j // 4, turn)
                    if j % 4 == 3:
                        conv_glu(j // 4, j // 4, turn)
                        c_low(j // 4, j // 4, turn)
            for k in range(KF):
                low(DOWN_C + SPL + k)
                if k == 2:
                    conv(NCH_FF - 1, 0)
                if k == 3:
                    conv_glu(NCH_FF - 1, 0)
                    c_low(NCH_FF - 1, 0)
            residual(END, None)
            square_1(7)
            v_.wait_ge(late_in[3], 16)
            for t in range(T):
                v_.wait_ge(rstd_ok, 2 * 7 + t + 1)
                ve.scalar_tensor_tensor(out=x[:, t], in0=x[:, t], scalar=stat[:, RSTD + t:RSTD + t + 1], in1=row[:],
                                        op0=ALU.mult, op1=ALU.mult).then_inc(out_ok, 1)

        @block.tensor
        def _(pe):
            mm = nc.tensor.matmul

            def wide(m, u, b, v, turn=None, wait_operand=False):
                if wait_operand:
                    pe.wait_ge(h_lo_ok, 4 * v + u + 1)
                pe.wait_ge(lo_done, at(m + 1, turn, LOOP))
                s = m % SPL
                for t in range(T):
                    o = bank[2 * b + t][:]
                    for k in range(2):
                        hi, lo = (h[:, 2 * u + k, t * P:(t + 1) * P] for h in (h_hi, h_lo))
                        mm(o, hi, w_hi[:, s, k], start=(u == 0 and k == 0), stop=False)
                        mm(o, hi, w_lo[:, s, k], start=False, stop=False)
                        last = mm(o, lo, w_hi[:, s, k], start=False, stop=(u == 3 and k == 1))
                last.then_inc(mm_done, 1)

            def tall(m, a_hi, a_lo, k, first, last_k, base=0, order=(0, 1), wait_zero=None):
                pe.wait_ge(lo_done, m + 1)
                s = m % SPL
                for n in order:
                    if n == 0 and wait_zero is not None:
                        pe.wait_ge(*wait_zero)
                    for t in range(T):
                        o = bank[base + 2 * n + t][:]
                        hi, lo = (h[:, k, t * P:(t + 1) * P] for h in (a_hi, a_lo))
                        mm(o, hi, w_hi[:, s, n], start=first, stop=False)
                        mm(o, hi, w_lo[:, s, n], start=False, stop=False)
                        last = mm(o, lo, w_hi[:, s, n], start=False, stop=last_k)
                last.then_inc(mm_done, 1)

            def transposes(v, src):
                for t in range(T):
                    pe.wait_ge((xn0, xn1)[t], v + 1)
                    for kk in range(4):
                        if t == 0 and kk == 3 and v in (4, 7, 8):
                            pe.wait_ge(xn1, v + 1)
                        for k in range(2):
                            last = nc.tensor.transpose(bank[4 + kk][:, k * S + t * P:k * S + (t + 1) * P],
                                                       src[:, t, (2 * kk + k) * P:(2 * kk + k + 1) * P], ident[:])
                        if t == T - 1:
                            last.then_inc(t_done, 1)

            def reduce_group(g, turn=None):
                pe.wait_ge(ada_done, at(8 * (g + 1), turn, 8))
                if g:
                    pe.wait_ge(ada_col, at(g, turn, 1))
                for q in range(4):
                    last = mm(bank[sum_bank(g)][:, q:q + 1], ada_acc[:, acc_slot(g), q * P:(q + 1) * P], ones[:, 0:1], start=True, stop=True)
                last.then_inc(ada_red, 1)

            def reduce_step(g, j, turn=None, steps=LOOP_REDUCE):
                if j in steps:
                    reduce_group(g + steps[j], turn)

            def gate(n, h):
                pe.wait_ge(gate_diag, 2 * n + h + 1)
                if 2 * n + h:
                    pe.wait_ge(gate_ok, 2 * n + h)
                mm(bank[7][:], ones[:], diag[:].rearrange("p k s -> p (k s)"), start=True, stop=True).then_inc(gate_mm, 1)

            pe.wait_ge(const_ok, 4)
            pe.wait_ge(c_load, 16)
            nc.tensor.transpose(bank[5][:, 0:KD], c_rows[:], ident[0:KD, 0:KD]).then_inc(setup_t, 1)
            reduce_group(0)
            pe.wait_ge(vec_in, 16 * VECS)
            nc.tensor.transpose(bank[7][:, 0:53], stage_v[0:53, 0, :], ident[0:53, 0:53])
            nc.tensor.transpose(bank[7][:, CONV_V:CONV_V + 88], stage_v[0:88, 1, :], ident[0:88, 0:88])
            nc.tensor.transpose(bank[7][:, ADAB_V:ADAB_V + 96], stage_v[0:96, 2, :], ident[0:96, 0:96]).then_inc(setup_t, 1)
            reduce_group(1)
            pe.wait_ge(setup_p, 1)
            for g in range(4):
                last = nc.tensor.transpose(bank[6][:, g * P:(g + 1) * P], w_sp[:, g], ident[:])
            last.then_inc(setup_t, 1)
            pe.wait_ge(setup, 3)
            transposes(0, xn)
            reduce_group(2)
            reduce_group(3)
            pe.wait_ge(ada_col, 4)
            for j in range(LOOP):
                wide(QKV_A + j, j % 4, j // 4, 0, wait_operand=True)
                reduce_step(4, j)

            def qk_transposes(n, f):
                if n >= 4:
                    pe.wait_ge((qk_d, qk_a)[n % 2], n // 2 - 1)
                for k in range(2):
                    for t in range(T):
                        last = nc.tensor.transpose(bank[4 + n % 4][:, k * S + t * P:k * S + (t + 1) * P],
                                                   proj[:, t, (2 * f + k) * P:(2 * f + k + 1) * P], ident[:])
                last.then_inc(qk_t, 1)

            for m in range(8, 24):
                if m in QK_STEPS_A:
                    pe.wait_ge(rope_ok, 1)
                    for n in (2 * (m - QK_STEPS_A[0]), 2 * (m - QK_STEPS_A[0]) + 1):
                        qk_transposes(n, QK_ORDER_A[n])
                if m % 4 == 0:
                    pe.wait_ge(evac, m // 4 - 1)
                wide(QKV_A + m, m % 4, m // 4 % 2, 0)
                if m == 23:
                    pe.wait_ge(qk_d, 4)
                    pe.wait_ge(qk_a, 4)
                reduce_step(4 + m // 8, m % 8)

            NH = 8
            for i in range(NH + 3):
                if i < NH:
                    if i == 0:
                        pe.wait_ge(evac, 5)
                    if i == 1:
                        pe.wait_ge(evac, 6)
                    if i >= 2:
                        pe.wait_ge(exp_ok, i - 1)
                    for c in range(2):
                        for t in range(T):
                            last = mm(bank[2 * (i % 2) + c][:, t * S:(t + 1) * S], qkT[64 * c:64 * c + 64, i, t * P:(t + 1) * P],
                                      qkT[64 * c:64 * c + 64, 8 + i, :], start=True, stop=True)
                    last.then_inc(sc_ok, 1)
                if i in (1, 2):
                    gate(0, i - 1)
                if 2 <= i < NH + 2:
                    h = i - 2
                    pe.wait_ge(wgt_ok, h + 1)
                    if h >= 2:
                        pe.wait_ge(wgt_ev, h - 1)
                    for t in range(T):
                        for k in range(2):
                            last = nc.tensor.transpose(bank[4 + h % 2][:, k * S + t * P:k * S + (t + 1) * P],
                                                       wgt[:, h % 2, t, k * P:(k + 1) * P], ident[:])
                    last.then_inc(wgt_t, 1)
                if i >= 3:
                    h = i - 3
                    pe.wait_ge(wgt_ev, h + 1)
                    if h == 0:
                        pe.wait_ge(ada_col, 7)
                        pe.wait_ge(gate_ok, 2)
                    if h >= 2:
                        pe.wait_ge(o_ok, h - 1)
                    for t in range(T):
                        for k in range(2):
                            last = mm(bank[6 + h % 2][:, t * P:(t + 1) * P], wgtT[:, h % 2, k, t * P:(t + 1) * P],
                                      proj[:, k, 2048 + h * P:2048 + (h + 1) * P], start=(k == 0), stop=(k == 1))
                    last.then_inc(pv_ok, 1)
            transposes(1, att)
            for k in range(KD):
                pe.wait_ge(h_lo_ok, 4 * 1 + (4 if k == 1 else k // 2 + 1))
                tall(WO_A + k, h_hi, h_lo, k, k == 0, k == KD - 1)
                reduce_step(7, k, steps={1: 0, 3: 1, 7: 2})
            pe.wait_ge(ada_col, 10)
            transposes(2, xn)

            def u_transpose(f, c, b, turn=None):
                pe.wait_ge(u_ok, at(NCH_FF * f + c + 1, turn, 2))
                for k in range(2):
                    for t in range(T):
                        last = nc.tensor.transpose(bank[4 + b][:, k * S + t * P:k * S + (t + 1) * P],
                                                   act_u[:, b, t, k * P:(k + 1) * P], ident[:])
                last.then_inc(u_t, 1)

            def feed_forward(base, f, v, gate_n, with_ada, out_g, out_n):
                for u in range(4):
                    wide(base + u, u, 0, v, wait_operand=True)
                with pe.Fori(0, 5) as turn:
                    for j in range(LOOP):
                        if j % 4 == 3:
                            u_transpose(f, j // 4, j // 4, turn)
                        wide(base + 4 + j, j % 4, 1 - j // 4, v, turn)
                        if with_ada:
                            reduce_step(10, j, turn)
                down = base + 4 * NCH_FF
                for k in range(KF):
                    if k == 3:
                        u_transpose(f, NCH_FF - 1, 0)
                    if k % 2 == 0:
                        pe.wait_ge(u_lo_ok, NCH_FF * f + k // 2 + 1)
                    tall(down + k, u_hi, u_lo, k, k == 0, k == KF - 1, order=(1, 0),
                         wait_zero=(u_ok, NCH_FF * (f + 1)) if k == 0 else None)
                    reduce_step(out_g, k, steps=first_steps(OUT_REDUCE, out_n))
                    if k in (14, 17):
                        gate(gate_n, (k - 14) // 3)

            feed_forward(IN_0, 0, 2, 1, True, 15, 4)
            transposes(3, xn)
            def qk_transposes_b(n, b):
                f = (4, 0, 1, 2, 3)[n]
                for k in range(2):
                    for t in range(T):
                        last = nc.tensor.transpose(bank[b][:, k * S + t * P:k * S + (t + 1) * P],
                                                   proj[:, t, (2 * f + k) * P:(2 * f + k + 1) * P], ident[:])
                last.then_inc(qk_t, 1)

            for m in range(12):
                if m == K_TURN_STEP_B:
                    pe.wait_ge(rope_ok, 2)
                    qk_transposes_b(0, 4)
                if m == 8:
                    pe.wait_ge(evac, 7)
                wide(QKV_B + m, m % 4, m // 4 % 2, 3, wait_operand=m < 4)
                reduce_step(19, m, steps=B_REDUCE)
                if m in (4, 9):
                    gate(2, (m - 4) // 5)
            pe.wait_ge(rope_ok, 3)
            qk_transposes_b(1, 5)
            pe.wait_ge(ada_col, 20)
            qk_transposes_b(2, 6)

            pe.wait_ge(qk_d, 6)
            pe.wait_ge(qk_a, 5)
            pe.wait_ge(evac, 9)
            def scores_b(i):
                if i >= 4:
                    pe.wait_ge(exp_ok, 8 + i - 3)
                for t in range(T):
                    last = mm(bank[i % 4][:, t * S:(t + 1) * S], qkT[:, i, t * P:(t + 1) * P], qkT[:, 8 + i // 4, :],
                              start=True, stop=True)
                last.then_inc(sc_ok, 1)

            def prob_transposes_b(h):
                pe.wait_ge(exp_ok, 8 + h + 1)
                if h >= 2:
                    pe.wait_ge(wgt_ev, 8 + h - 1)
                for t in range(T):
                    for k in range(2):
                        last = nc.tensor.transpose(bank[4 + h % 2][:, k * S + t * P:k * S + (t + 1) * P],
                                                   prob_b[:, h % 2, t, k * P:(k + 1) * P], ident[:])
                last.then_inc(wgt_t, 1)

            def times_v_b(h):
                pe.wait_ge(wgt_ev, 8 + h + 1)
                if h == 0:
                    pe.wait_ge(gate_ok, 6)
                if h >= 2:
                    pe.wait_ge(o_ok, 8 + h - 1)
                v0 = 1280 + h // 4 * P
                for t in range(T):
                    for k in range(2):
                        last = mm(bank[6 + h % 2][:, t * P:(t + 1) * P], probT_b[:, h % 2, k, t * P:(t + 1) * P],
                                  proj[:, k, v0:v0 + P], start=(k == 0), stop=(k == 1))
                last.then_inc(pv_ok, 1)

            for i in range(NH + 3):
                if i == 4:
                    prob_transposes_b(2)
                    times_v_b(1)
                    pe.wait_ge(rope_ok, 4)
                    pe.wait_ge(exp_ok, 8 + 3)
                    qk_transposes_b(3, 2)
                    pe.wait_ge(exp_ok, 8 + 4)
                    qk_transposes_b(4, 3)
                    prob_transposes_b(3)
                    times_v_b(2)
                    pe.wait_ge(qk_d, 7)
                    pe.wait_ge(qk_a, 6)
                if i < NH:
                    scores_b(i)
                if 2 <= i < NH + 2 and i not in (4, 5):
                    prob_transposes_b(i - 2)
                if i in (3, 7, 8, 9, 10):
                    times_v_b(i - 3)
                if i == 5:
                    times_v_b(3)
            transposes(4, att_b)
            for k in range(KD):
                pe.wait_ge(h_lo_ok, 4 * 4 + (4 if k == 2 else k // 2 + 1))
                tall(WO_B + k, h_hi, h_lo, k, k == 0, k == KD - 1)
                reduce_step(20, k, steps={2: 0, 6: 1})
            transposes(5, xn)
            feed_forward(IN_1, 1, 5, 3, False, 22, 2)

            transposes(6, xn)
            with pe.Fori(0, 3) as turn:
                for j in range(LOOP):
                    if j % 4 == 0:
                        pe.wait_ge(evac, at(9 + j // 4 - 1, turn, 2))
                    wide(IN_C + j, j % 4, j // 4, 6, turn, wait_operand=True)

            def qk_transposes(f):
                if f >= 4:
                    pe.wait_ge((c_qkd, c_qka)[f % 2], f // 2 - 1)
                for k in range(2):
                    for t in range(T):
                        last = nc.tensor.transpose(bank[4 + f % 4][:, k * S + t * P:k * S + (t + 1) * P],
                                                   proj[:, t, 1536 + (2 * f + k) * P:1536 + (2 * f + k + 1) * P], ident[:])
                last.then_inc(c_qkt, 1)

            def spatial():
                pe.wait_ge(gm_v, 1)
                for t in range(T):
                    for g in range(4):
                        last = mm(bank[4 + 2 * t + g // 2][:, g % 2 * 192:g % 2 * 192 + 192], w_spT[:, g],
                                  proj[:, t, 768 + 192 * g:768 + 192 * g + 192], start=True, stop=True)
                last.then_inc(gm_mm, 1)

            def scores(i):
                if i >= 1:
                    pe.wait_ge(c_sm, i)
                else:
                    pe.wait_ge(evac, 9 + 8)
                    pe.wait_ge(c_qkd, 3)
                    pe.wait_ge(c_qka, 3)
                r0 = i % 2 * 64
                for g in range(3):
                    q = (4 * g + i) // 2
                    for t, width in enumerate((P, S)):
                        last = mm(bank[2 + g][:, t * S:t * S + width], qkT[r0:r0 + 64, q, t * P:(t + 1) * P],
                                  qkT[r0:r0 + 64, 6 + q, 0:width], start=True, stop=True)
                last.then_inc(c_sc, 1)

            tiles = [(0, g, 0, g * P) for g in range(3)]
            tiles += [(1, g, k, 384 + g * S + k * P) for g in range(3) for k in range(2)]

            def prob_transposes(h):
                pe.wait_ge(c_exp, h + 1)
                if h >= 1:
                    pe.wait_ge(c_o, h)
                for n, (t, g, k, c0) in enumerate(tiles):
                    last = nc.tensor.transpose(bank[5 + n // 4][:, n % 4 * P:(n % 4 + 1) * P], prob_c[:, h % 2, c0:c0 + P],
                                               ident[:])
                last.then_inc(c_pt, 1)

            def times_v(h):
                pe.wait_ge(c_pev, h + 1)
                for n, (t, g, k, c0) in enumerate(tiles):
                    v0 = 3072 + 64 * (4 * g + h)
                    last = mm(bank[7][:, 256 + t * 64:320 + t * 64], probT_c[:, n], proj[:, k, v0:v0 + 64],
                              start=(n in (0, 3)), stop=(n in (2, 8)))
                last.then_inc(c_pv, 1)

            for m in range(24, 47):
                if m == QK_STEPS[0]:
                    pe.wait_ge(rope_ok, 5)
                    pe.wait_ge(gm_y, 1)
                if m in QK_STEPS:
                    qk_transposes(2 * (m - QK_STEPS[0]))
                    qk_transposes(2 * (m - QK_STEPS[0]) + 1)
                if m == SPATIAL_STEP:
                    spatial()
                if m in SCORE_STEPS:
                    scores(SCORE_STEPS.index(m))
                if m in PROBT_STEPS:
                    prob_transposes(PROBT_STEPS.index(m))
                if m in PV_STEPS:
                    times_v(PV_STEPS.index(m))
                if m % 4 == 0 and m <= 44:
                    pe.wait_ge(evac, 9 + (m // 4 - 1 if m <= 32 else m // 4))
                if m < 44:
                    wide(IN_C + m, m % 4, c_bank(m // 4), 6)
                elif m < 46:
                    j = m - 44
                    pe.wait_ge(lo_done, IN_C + m + 1)
                    s = (IN_C + m) % SPL
                    whi, wlo = (w[:, s].rearrange("p a (b n) -> p (a b) n", b=2) for w in (w_hi, w_lo))
                    for t in range(T):
                        o = bank[t][:, 0:HC]
                        for k in range(4):
                            hi, lo = (h[:, 4 * j + k, t * P:(t + 1) * P] for h in (h_hi, h_lo))
                            mm(o, hi, whi[:, k], start=(j == 0 and k == 0), stop=False)
                            mm(o, hi, wlo[:, k], start=False, stop=False)
                            last = mm(o, lo, whi[:, k], start=False, stop=(j == 1 and k == 3))
                    last.then_inc(mm_done, 1)
            transposes(7, y_c)
            for k in range(6):
                pe.wait_ge(h_lo_ok, 4 * 7 + k // 2 + 1)
                tall(BR_A + k, h_hi, h_lo, k, k == 0, k == 5)
            pe.wait_ge(h_lo_ok, 4 * 7 + 4)
            for k in range(2):
                tall(BR_B + k, h_hi, h_lo, 6 + k, k == 0, k == 1, base=4)
            transposes(8, merged)
            for k in range(KD):
                pe.wait_ge(h_lo_ok, 4 * 8 + k // 2 + 1)
                tall(OUT_C + k, h_hi, h_lo, k, k == 0, k == KD - 1)
            transposes(9, xn)

            def av_transpose(c, b, turn=None):
                pe.wait_ge(av_ok, at(c + 1, turn, 2))
                for half_, bk in enumerate((4 + b, 6 + b)):
                    for k in range(2):
                        for t in range(T):
                            c0 = half_ * HC + k * P
                            last = nc.tensor.transpose(bank[bk][:, k * S + t * P:k * S + (t + 1) * P], av[:, b, t, c0:c0 + P],
                                                       ident[:])
                last.then_inc(av_t, 1)

            for u in range(4):
                wide(UP_C + u, u, 0, 9, wait_operand=True)
            with pe.Fori(0, 5) as turn:
                for j in range(LOOP):
                    if j % 4 == 2:
                        av_transpose(j // 4, j // 4, turn)
                    wide(UP_C + 4 + j, j % 4, 1 - j // 4, 9, turn)
            for k in range(KF):
                if k == 2:
                    av_transpose(NCH_FF - 1, 0)
                if k % 2 == 0:
                    pe.wait_ge(c_lo, k // 2 + 1)
                tall(DOWN_C + k, u_hi, u_lo, k, k == 0, k == KF - 1, order=(1, 0),
                     wait_zero=(av_ok, NCH_FF) if k == 0 else None)


_INPUTS = ["x", "c", "ada_w", "ada_b", "norm1_g", "norm2_g", "a_w_qkv", "a_w_o", "a_lam_q1", "a_lam_k1", "a_lam_q2",
           "a_lam_k2", "a_subln_g", "b_w_qkv", "b_w_o", "b_qnorm_g", "b_knorm_g", "f_w_in", "f_w_out", "final_g",
           "positions_2", "mix_norm_g_2", "w_in_2", "gmlp_norm_g_2", "w_spatial_2", "b_spatial_2", "w_branch_a_2",
           "w_branch_b_2", "w_out_2", "ffn_norm_g_2", "w_up_2", "conv_w_2", "conv_b_2", "w_down_2", "final_norm_g_2"]


def constants():
    f = np.float32

    def angles(pos, half, theta):
        freqs = (f(theta) ** (-np.arange(half, dtype=f) / f(half))).astype(f)
        a = (pos.astype(f)[:, None] * freqs[None, :]).astype(f)
        return np.cos(a).astype(f), np.sin(a).astype(f)

    tok = np.arange(S)
    cos, sin = angles(tok, 8, 500000.0)
    rope_a = np.stack([np.concatenate([cos, cos], 1), np.concatenate([-sin, sin], 1)], 1)
    cr, sr = angles(tok // 64, 32, 10000.0)
    cc, sc = angles(tok % 64, 32, 10000.0)
    rope_b = np.stack([np.concatenate([cr, cr, cc, cc], 1), np.concatenate([-sr, sr, -sc, sc], 1)], 1)
    inv_freq = (f(500000.0) ** (-np.arange(0, 16, 2, dtype=f) / f(16))).astype(f)
    i, j = tok[:, None], tok[None, :]
    seen = [(i >= j) & (i - j <= 128 * d) & ((i - j) % d == 0) for d in (1, 4, 16)]
    far = [np.where(m, 0.0, -3e37).astype(f) for m in seen]
    masks = np.concatenate([m[:P, :P] for m in far] + [m[P:, :] for m in far], 1)
    return {"rope_a": rope_a.astype(f), "rope_b": rope_b.astype(f), "inv_freq": inv_freq, "masks": masks}


def kernel(**inputs):
    import concourse.bacc as bacc
    from concourse.bass_utils import run_bass_kernel_spmd

    nc = bacc.Bacc("TRN2", target_bir_lowering=False, num_devices=1)
    arrays, args = {}, []
    for name, a in [(n, np.ascontiguousarray(inputs[n])) for n in _INPUTS] + list(constants().items()):
        arrays["in_" + name] = a
        args.append(nc.dram_tensor("in_" + name, a.shape, mybir.dt.from_np(a.dtype), kind="ExternalInput").ap())
    out = nc.dram_tensor("out", (1, S, D), F32, kind="ExternalOutput").ap()
    program(nc, *args, out)
    r = run_bass_kernel_spmd(nc, [arrays], core_ids=[0])
    return r.results[0]["out"]
```
